# Optimizing a Trainium2 kernel written in Bass

```python
import math
import jax, jax.numpy as jnp
from jax import lax
import numpy as np

D_MODEL = 1024
BATCH = 1
SEQ = 512
DEPTH = 1

EPS = 1e-6
CONV_CH = 512
CONV_K = 31
N_HEADS = 8
HEAD_DIM = 64
ATT_W = N_HEADS * HEAD_DIM
N_IDX_HEADS = 4
IDX_DIM = 64
TOPK_MAX = 256
Q_BLOCK = 128
NUM_BUCKETS = 32
MAX_DISTANCE = 128
SSM_HEADS = 8
SSM_HEAD_DIM = 64
SSM_INNER = SSM_HEADS * SSM_HEAD_DIM
SSM_GROUPS = 2
SSM_STATE = 128
SSM_CONV_K = 4
SSM_XBC = SSM_INNER + 2 * SSM_GROUPS * SSM_STATE
CHUNK = 128
D_MIX = CONV_CH + ATT_W + SSM_INNER
COL_SIZES = [CONV_CH, CONV_CH,
             ATT_W, ATT_W, ATT_W,
             N_IDX_HEADS * IDX_DIM, IDX_DIM, N_IDX_HEADS,
             SSM_INNER, SSM_XBC, SSM_HEADS]
SPLITS = [int(v) for v in np.cumsum(COL_SIZES)[:-1]]
D_IN = int(sum(COL_SIZES))
D_FF = 2816
FFN_CONV_K = 3

kernel_name = "hybrid_conv_dsa_ssd_block"

def rms_norm(x, g):
    xf = x.astype(jnp.float32)
    y = xf * lax.rsqrt(jnp.mean(xf * xf, axis=-1, keepdims=True) + EPS)
    return (y * g.astype(jnp.float32)).astype(x.dtype)

def layer_norm(x, g, b):
    xf = x.astype(jnp.float32)
    mu = jnp.mean(xf, axis=-1, keepdims=True)
    var = jnp.mean(jnp.square(xf - mu), axis=-1, keepdims=True)
    y = (xf - mu) * lax.rsqrt(var + EPS)
    return (y * g.astype(jnp.float32) + b.astype(jnp.float32)).astype(x.dtype)

def causal_dwconv(u, w, b):
    k_w, c = w.shape
    y = lax.conv_general_dilated(
        u, w[:, None, :].astype(u.dtype), window_strides=(1,), padding=[(k_w - 1, 0)],
        dimension_numbers=("NWC", "WIO", "NWC"), feature_group_count=c)
    return y + b.astype(u.dtype)

def t5_bucket(rel):
    n = jnp.maximum(rel, 0)
    max_exact = NUM_BUCKETS // 2
    nf = jnp.maximum(n, 1).astype(jnp.float32)
    large = max_exact + (jnp.log(nf / max_exact) / math.log(MAX_DISTANCE / max_exact)
                         * (NUM_BUCKETS - max_exact)).astype(jnp.int32)
    large = jnp.minimum(large, NUM_BUCKETS - 1)
    return jnp.where(n < max_exact, n, large)

def sparse_attention(q, k, v, iq, ik, iw, rel_bias):
    bsz, s_len = q.shape[0], q.shape[1]
    topk = min(TOPK_MAX, s_len // 4)
    n_blocks = s_len // Q_BLOCK
    s_pos = jnp.arange(s_len)

    def block(i):
        q0 = i * Q_BLOCK
        qb = lax.dynamic_slice_in_dim(q, q0, Q_BLOCK, 1)
        iqb = lax.dynamic_slice_in_dim(iq, q0, Q_BLOCK, 1)
        iwb = lax.dynamic_slice_in_dim(iw, q0, Q_BLOCK, 1)
        t_pos = q0 + jnp.arange(Q_BLOCK)
        dots = jnp.einsum("bqhd,bsd->bqsh", iqb, ik) * (IDX_DIM ** -0.5)
        score = jnp.einsum("bqsh,bqh->bqs", jax.nn.relu(dots), iwb) * (N_IDX_HEADS ** -0.5)
        causal = s_pos[None, :] <= t_pos[:, None]
        score = jnp.where(causal[None], score.astype(jnp.float32), -jnp.inf)
        _, idx = lax.top_k(score, topk)
        kg = jax.vmap(lambda kk, ii: kk[ii])(k, idx)
        vg = jax.vmap(lambda vv, ii: vv[ii])(v, idx)
        logits = jnp.einsum("bqhd,bqkhd->bqhk", qb, kg).astype(jnp.float32) * (HEAD_DIM ** -0.5)
        rel = t_pos[None, :, None] - idx
        bias = rel_bias[t5_bucket(rel)].astype(jnp.float32)
        logits = logits + jnp.transpose(bias, (0, 1, 3, 2))
        logits = jnp.where((rel >= 0)[:, :, None, :], logits, -jnp.inf)
        p = jax.nn.softmax(logits, axis=-1).astype(v.dtype)
        return jnp.einsum("bqhk,bqkhd->bqhd", p, vg)

    out = lax.map(block, jnp.arange(n_blocks))
    return jnp.transpose(out, (1, 0, 2, 3, 4)).reshape(bsz, s_len, ATT_W)

def ssd_scan(xh, dt, a, bm, cm):
    bsz, s_len, n_h, p_dim = xh.shape
    n_c = s_len // CHUNK
    rep = n_h // SSM_GROUPS
    bh = jnp.repeat(bm, rep, axis=2).reshape(bsz, n_c, CHUNK, n_h, SSM_STATE)
    ch = jnp.repeat(cm, rep, axis=2).reshape(bsz, n_c, CHUNK, n_h, SSM_STATE)
    xd = (xh.astype(jnp.float32) * dt[..., None]).reshape(bsz, n_c, CHUNK, n_h, p_dim)
    cs = jnp.cumsum((dt * a).reshape(bsz, n_c, CHUNK, n_h), axis=2)
    seg = cs[:, :, :, None, :] - cs[:, :, None, :, :]
    tri = jnp.tril(jnp.ones((CHUNK, CHUNK), dtype=bool))
    decay_ls = jnp.exp(jnp.where(tri[None, None, :, :, None], seg, -jnp.inf))
    scores = jnp.einsum("bclhn,bcshn->bclsh", ch, bh).astype(jnp.float32) * decay_ls
    y_diag = jnp.einsum("bclsh,bcshp->bclhp", scores, xd)
    decay_end = jnp.exp(cs[:, :, -1:, :] - cs)
    states = jnp.einsum("bclhn,bclh,bclhp->bchpn", bh.astype(jnp.float32), decay_end, xd)
    chunk_decay = jnp.exp(cs[:, :, -1, :])

    def step(h, inp):
        st, dec = inp
        return h * dec[:, :, None, None] + st, h

    h0 = jnp.zeros((bsz, n_h, p_dim, SSM_STATE), jnp.float32)
    _, prev = lax.scan(step, h0, (jnp.moveaxis(states, 1, 0), jnp.moveaxis(chunk_decay, 1, 0)))
    prev = jnp.moveaxis(prev, 0, 1)
    y_off = jnp.einsum("bclhn,bchpn,bclh->bclhp", ch.astype(jnp.float32), prev, jnp.exp(cs))
    return (y_diag + y_off).reshape(bsz, s_len, n_h, p_dim)

def setup_inputs(seed: int = 0) -> dict:
    key = jax.random.key(seed)
    ks = jax.random.split(key, 24)
    f32 = jnp.float32
    nrm = lambda k, shape, scale: jax.random.normal(k, shape, f32) * scale
    gain = lambda k, shape: 1.0 + 0.05 * jax.random.normal(k, shape, f32)
    dt0 = jnp.exp(jax.random.uniform(ks[14], (DEPTH, SSM_HEADS), f32, math.log(1e-3), math.log(1e-1)))
    return {
        "x": jax.random.normal(ks[0], (BATCH, SEQ, D_MODEL), f32),
        "rel_bias": nrm(ks[1], (NUM_BUCKETS, N_HEADS), 0.1),
        "norm_mix_g": gain(ks[2], (DEPTH, D_MODEL)),
        "w_in": nrm(ks[3], (DEPTH, D_MODEL, D_IN), D_MODEL ** -0.5),
        "conv_dw_w": nrm(ks[4], (DEPTH, CONV_K, CONV_CH), CONV_K ** -0.5),
        "conv_dw_b": nrm(ks[5], (DEPTH, CONV_CH), 0.02),
        "conv_ln_g": gain(ks[6], (DEPTH, CONV_CH)),
        "conv_ln_b": nrm(ks[7], (DEPTH, CONV_CH), 0.02),
        "q_norm_g": gain(ks[8], (DEPTH, HEAD_DIM)),
        "k_norm_g": gain(ks[9], (DEPTH, HEAD_DIM)),
        "ssm_conv_w": nrm(ks[10], (DEPTH, SSM_CONV_K, SSM_XBC), SSM_CONV_K ** -0.5),
        "ssm_conv_b": nrm(ks[11], (DEPTH, SSM_XBC), 0.02),
        "dt_bias": dt0 + jnp.log(-jnp.expm1(-dt0)),
        "a_log": jnp.log(jax.random.uniform(ks[12], (DEPTH, SSM_HEADS), f32, 1.0, 16.0)),
        "d_skip": gain(ks[13], (DEPTH, SSM_HEADS)),
        "ssm_norm_g": gain(ks[15], (DEPTH, SSM_INNER)),
        "w_out": nrm(ks[16], (DEPTH, D_MIX, D_MODEL), D_MIX ** -0.5),
        "norm_ffn_g": gain(ks[17], (DEPTH, D_MODEL)),
        "w_up": nrm(ks[18], (DEPTH, D_MODEL, 2 * D_FF), D_MODEL ** -0.5),
        "ffn_conv_w": nrm(ks[19], (DEPTH, FFN_CONV_K, 2 * D_FF), FFN_CONV_K ** -0.5),
        "ffn_conv_b": nrm(ks[20], (DEPTH, 2 * D_FF), 0.02),
        "w_down": nrm(ks[21], (DEPTH, D_FF, D_MODEL), D_FF ** -0.5),
    }

def reference(x, rel_bias, norm_mix_g, w_in, conv_dw_w, conv_dw_b, conv_ln_g, conv_ln_b,
              q_norm_g, k_norm_g, ssm_conv_w, ssm_conv_b, dt_bias, a_log, d_skip, ssm_norm_g,
              w_out, norm_ffn_g, w_up, ffn_conv_w, ffn_conv_b, w_down):
    bsz, s_len, _ = x.shape
    for i in range(DEPTH):
        h = rms_norm(x, norm_mix_g[i])
        proj = h @ w_in[i]
        ca, cg, q, k, v, iq, ik, iw, z, xbc, dt = jnp.split(proj, SPLITS, axis=-1)

        u = ca * jax.nn.sigmoid(cg)
        u = causal_dwconv(u, conv_dw_w[i], conv_dw_b[i])
        u = jax.nn.silu(layer_norm(u, conv_ln_g[i], conv_ln_b[i]))

        qh = rms_norm(q.reshape(bsz, s_len, N_HEADS, HEAD_DIM), q_norm_g[i])
        kh = rms_norm(k.reshape(bsz, s_len, N_HEADS, HEAD_DIM), k_norm_g[i])
        vh = v.reshape(bsz, s_len, N_HEADS, HEAD_DIM)
        att = sparse_attention(qh, kh, vh,
                               iq.reshape(bsz, s_len, N_IDX_HEADS, IDX_DIM), ik, iw, rel_bias)

        xbc = jax.nn.silu(causal_dwconv(xbc, ssm_conv_w[i], ssm_conv_b[i]))
        xs, bm, cm = jnp.split(xbc, [SSM_INNER, SSM_INNER + SSM_GROUPS * SSM_STATE], axis=-1)
        xs_h = xs.reshape(bsz, s_len, SSM_HEADS, SSM_HEAD_DIM)
        dtf = jax.nn.softplus(dt.astype(jnp.float32) + dt_bias[i].astype(jnp.float32))
        a = -jnp.exp(a_log[i].astype(jnp.float32))
        y = ssd_scan(xs_h, dtf, a,
                     bm.reshape(bsz, s_len, SSM_GROUPS, SSM_STATE),
                     cm.reshape(bsz, s_len, SSM_GROUPS, SSM_STATE))
        y = (y + d_skip[i].astype(jnp.float32)[:, None] * xs_h.astype(jnp.float32)).astype(x.dtype)
        y = rms_norm(y.reshape(bsz, s_len, SSM_INNER) * jax.nn.silu(z), ssm_norm_g[i])

        x = x + jnp.concatenate([u, att, y], axis=-1) @ w_out[i]

        h = rms_norm(x, norm_ffn_g[i])
        f = causal_dwconv(h @ w_up[i], ffn_conv_w[i], ffn_conv_b[i])
        fa, fg = jnp.split(f, 2, axis=-1)
        x = x + (jax.nn.silu(fg) * fa) @ w_down[i]
    return x


_drawn_inputs = setup_inputs


def setup_inputs(seed=0):
    import zlib

    import numpy as np

    out = dict(_drawn_inputs(seed))
    spreads = {}
    factors = {'rel_bias': 7.377,
     'conv_dw_b': 4.379,
     'conv_ln_g': 2.891,
     'conv_ln_b': 8.0,
     'q_norm_g': 8.0,
     'k_norm_g': 8.0,
     'ssm_conv_b': 3.871,
     'd_skip': 4.747,
     'ffn_conv_b': 4.471}
    for name, (base, spread) in spreads.items():
        noise = np.random.default_rng([zlib.crc32(name.encode()), seed]).standard_normal(out[name].shape)
        drawn = base * np.exp(spread * noise) if base else spread * noise
        out[name] = __import__('jax').numpy.asarray(drawn.astype(out[name].dtype))
    for name, factor in factors.items():
        out[name] = (out[name] * factor).astype(out[name].dtype)
    return out
```

```python
from contextlib import ExitStack

import numpy as np

import concourse.bass as bass
from concourse import mybir

ALU = mybir.AluOpType
ACT = mybir.ActivationFunctionType
AX_X = mybir.AxisListType.X
F32 = mybir.dt.float32
F32R = mybir.dt.float32r
BF16 = mybir.dt.bfloat16

P = 128
SEQ, DM = 512, 1024
NT = SEQ // P
KD = DM // P
EPS = 1e-6
CONV_CH, CONV_K = 512, 31
NH, HD = 8, 64
NIH, ID = 4, 64
TOPK = 128
NBUCKET, MAXDIST = 32, 128
SH, SP_, SG, SN, SK = 8, 64, 2, 128, 4
D_FF, FK = 2816, 3
NF = D_FF // P
COLS = np.cumsum([0, CONV_CH, CONV_CH, 512, 512, 512, NIH * ID, ID, NIH, 512, 1024, SH])
C_CA, C_CG, C_Q, C_K, C_V, C_IQ, C_IK, C_IW, C_Z, C_XBC, C_DT = [int(v) for v in COLS[:-1]]
MASKED = -3.0e38
TAKEN = -3.3e38
NG = 640

R_GM, R_GF, R_CB, R_LG, R_LB, R_SW, R_SB, R_FB = 0, 8, 16, 20, 24, 28, 60, 68
R_QG, R_KG = 112, 113
N_ROW0 = 114
R_CW = N_ROW0
R_FW = R_CW + CONV_K * 4
N_PRM = R_FW + FK * 2 * NF

CHUNKS = [("iq", 0)] + [("conv", j) for j in range(4)]
for what in "qkv":
    CHUNKS += [(what, 0), (what, 1)]
CHUNKS += [("xbc", j) for j in range(4)] + [("z", 0), ("z", 1)]
CHUNKS += [("out", (g, half)) for g in ("att", "conv", "ssm") for half in range(2)]
UP0 = len(CHUNKS)
CHUNKS += [("up", j) for j in range(NF)]
DN0 = len(CHUNKS)
CHUNKS += [("down", j) for j in range(NF // 2)]
AT = {c: n for n, c in enumerate(CHUNKS)}
NSLOT = 2
MIX_TILE = {"conv": 0, "att": 4, "ssm": 8}


def bucket_onehot():
    n = np.maximum(511 - np.arange(NG), 0)
    nf = np.maximum(n, 1).astype(np.float32)
    half = NBUCKET // 2
    large = half + (np.log(nf / np.float32(half)) / np.float32(np.log(MAXDIST / half))
                    * np.float32(NBUCKET - half)).astype(np.int32)
    b = np.where(n < half, n, np.minimum(large, NBUCKET - 1))
    return (np.arange(NBUCKET)[:, None] == b[None, :]).astype(np.float32)


def make_plan():
    plan = [("prm",), ("norm1",)]
    plan += [("hT", k) for k in range(KD)]
    plan += [("small",), ("mm", 0), ("dtprep",), ("gtab",), ("split", 1)]
    idx = [("idx", b, h) for b in (1, 2, 3) for h in range(NIH)]
    plan += [("mm", 1), ("split", 2), ("glu", 0)] + idx[:4] + [("topk", 1, 0, 8)]
    plan += [("mm", 2), ("split", 3), ("glu", 1)] + idx[4:8] + [("topk", 1, 8, 16)]
    plan += [("mm", 3), ("split", 4), ("glu", 2)] + [("dw", 0, 0, 16)]
    plan += [("mm", 4), ("split", 5), ("glu", 3)] + [("tbias", h) for h in range(NH)] + [("dw", 0, 16, 31)]
    plan += [("mm", 5), ("split", 6), ("topk", 2, 0, 8)]
    plan += [("mm", 6), ("split", 7), ("qkev", "q"), ("topk", 2, 8, 16)]
    plan += idx[8:]
    plan += [("mm", 7), ("split", 8), ("qkn", "q"), ("topk", 3, 0, 8)]
    plan += [("mm", 8), ("split", 9), ("qkev", "k"), ("topk", 3, 8, 16)]
    plan += [("mm", 9), ("split", 10), ("qkn", "k"), ("qkT", "q"), ("dw", 1, 0, 16)]
    plan += [("mm", 10), ("split", 11), ("qkT", "k"), ("vev",), ("dw", 1, 16, 31)]
    heads = [(b, h) for b in range(NT) for h in range(NH)]
    att = []
    for i in range(len(heads) + 2):
        if i < len(heads):
            att.append(("score", i, *heads[i]))
        if 1 <= i <= len(heads):
            att.append(("turn", i - 1, *heads[i - 1]))
        if i >= 2:
            att.append(("pv", i - 2, *heads[i - 2]))
            if heads[i - 2][1] == NH - 1:
                att.append(("attout", heads[i - 2][0]))
    cut = [len(att) * n // 6 for n in range(7)]
    for n in range(6):
        c = 11 + n
        plan += [("mm", c), ("split", c + 1)]
        plan += [("xbc", n)] if n < 4 else [("zev",)] if n == 5 else []
        plan += att[cut[n]:cut[n + 1]]
    plan += [("dw", 2, 0, 31)]
    plan += [("xt", t) for t in range(NT)] + [("cs",)]
    for t in range(NT):
        plan += [("ssd", t), ("dw", 3, 8 * t, min(8 * t + 8, 31)), ("ssdout", t), ("ssdT", t)]
    plan += [("ln", t) for t in range(NT)] + [("lnT", j) for j in range(4)]
    for n in range(6):
        plan += [("mm", 17 + n), ("split", 18 + n)]
    return plan


PLAN = make_plan()


def make_groups():
    acc, aux, out, step = [], [], [], {}
    n = n_out = 0

    def group(*key):
        nonlocal n
        acc.append(key)
        n += 1
        step[key] = n

    for s in PLAN:
        k = s[0]
        if k in ("prm", "hT", "tbias", "idx", "score", "turn", "ln", "lnT"):
            aux.append(s)
        elif k == "small":
            group("ik")
            group("iwdt")
        elif k == "gtab":
            aux += [("gt", 0), ("gt", 1)]
        elif k == "qkT":
            aux += [("qkT", s[1], j) for j in range(4)]
        elif k == "pv":
            n_out += 1
            if s[3] == 0:
                out.append(("pv", s[2]))
            step[("pv", s[2])] = n_out
        elif k == "xt":
            aux.append(("xs", s[1]))
        elif k == "cs":
            aux.append(("cs",))
        elif k == "ssd":
            aux += [("csr", s[1], 0), ("csr", s[1], 1), ("gt2", s[1])]
            if s[1] < NT - 1:
                aux.append(("bt", s[1]))
        elif k == "ssdout":
            out.append(("yd", s[1]))
            n_out += 1
            step[("yd", s[1])] = n_out
            if s[1] > 0:
                aux.append(("yo", s[1]))
            if s[1] < NT - 1:
                aux.append(("st", s[1]))
        elif k == "ssdT":
            aux.append(("yT", s[1]))
        elif k == "mm":
            what, i = CHUNKS[s[1]]
            if what in ("iq", "xbc"):
                group(what, 2 * i)
                group(what, 2 * i + 1)
            elif what == "conv":
                group("cg", i)
                group("ca", i)
            elif what in "qkvz":
                if i == 0:
                    acc += [(what, t) for t in range(NT)]
                    n += 1
                else:
                    for t in range(NT):
                        n += 1
                        step[(what, t)] = n
            elif what == "out":
                for t in range(NT):
                    group("wo", *i, t)
            step[("chunk", s[1])] = n
    return acc, aux, out, step, n


ACC, AUX, OUT, STEP, STEP0 = make_groups()
for j in range(NF):
    STEP[("chunk", UP0 + j)] = STEP0 + 2 * (j + 1)
for j in range(NF // 2):
    STEP[("chunk", DN0 + j)] = STEP0 + 2 * NF + j + 1
HIGH = [s for s in PLAN if s[0] in ("hT", "attout", "ssdT")]
SEL0 = {1: 0, 2: 256, 3: 640}
assert len(ACC) % 4 == 0
ROUND0 = len(ACC) // 4
AUX += [("h2T", k) for k in range(KD)]
RING = {}
for ring, groups, first, count in (("acc", ACC, 0, 4), ("aux", AUX, 4, 3), ("out", OUT, 7, 1)):
    for n, g in enumerate(groups):
        RING[g] = (ring, n, first + n % count, n // count)
DRAINS = [ROUND0] * 4 + [sum(RING[g][2] == b for g in AUX) for b in (4, 5, 6)] + [len(OUT)]


def build(nc, x, rel_bias, norm_mix_g, w_in, conv_dw_w, conv_dw_b, conv_ln_g, conv_ln_b, q_norm_g,
          k_norm_g, ssm_conv_w, ssm_conv_b, dt_bias, a_log, d_skip, ssm_norm_g, w_out, norm_ffn_g,
          w_up, ffn_conv_w, ffn_conv_b, w_down, onehot, out):
    x, out = x[0], out[0]
    w_in, w_out, w_up, w_down = w_in[0], w_out[0], w_up[0], w_down[0]
    gdram = nc.dram_tensor("distance_table", (NH, NG), F32, kind="Internal").ap()

    with ExitStack() as ctx:
        base = (nc.sbuf_base + 63) // 64 * 64
        top = [base]

        def at(name, shape, dt, offset=None):
            size = (int(np.prod(shape[1:])) * (2 if dt == BF16 else 4) + 31) // 32 * 32
            if offset is None:
                offset = top[0]
                top[0] += size
            return nc.alloc_sbuf_tensor_at(name, shape, dt, offset=offset)

        def region(kb):
            o = top[0]
            top[0] += int(kb * 1024)
            return o

        K = 1024
        ident = at("ident", [P, P], F32)
        tri = at("tri", [P, P], F32)
        neg_l = at("neg_l", [P, P], F32)
        neg_q = at("neg_q", [P, P], F32)
        ones = at("ones", [P, P], F32)
        prm = at("prm", [P, N_PRM], F32)
        st = at("stats", [P, 816], F32)
        wraw = at("w_raw", [P, NSLOT, 2048], F32)
        whi = at("w_hi", [P, NSLOT, 2048], F32R)
        wlo = at("w_lo", [P, NSLOT, 2048], F32R)
        hhi = at("h_hi", [P, KD, SEQ], F32R)
        hlo = at("h_lo", [P, KD, SEQ], F32R)
        r1 = region(16)
        mix0 = top[0]
        r2, r3, r4, r5, r6, r7, rs = (region(kb) for kb in (16, 16, 16, 10.5, 16, 16, 8))
        x_sb = at("x_in", [P, NT, DM], F32, r2)
        xn = at("x_normed", [P, NT, DM], F32, r6)
        rows = at("param_rows", [P, 4, P], F32, rs)
        ws_raw = at("small_raw", [P, KD, 140], F32, r4)
        ws_hi = at("small_hi", [P, KD, 140], F32R, r4 + 4608)
        ws_lo = at("small_lo", [P, KD, 140], F32R, r4 + 9216)
        oneh = at("onehot_sb", [NBUCKET, NG], F32, r1)
        relb = at("relb", [NBUCKET, NH], F32, r1 + 2560)
        gsb = at("gsb", [NH, NG], F32, r1 + 3 * K)
        jrev = at("jrev", [P, P], F32, r1 + 6 * K)
        trev = at("trev", [P, NH, 512], F32, r6)
        tbias = at("tbias", [P, NH, 512], F32, r2)
        iqT = at("iqT", [P, 2, SEQ], F32, r3)
        ikT = at("ikT", [P, SEQ], F32, r3 + 4 * K)
        relu = at("relu", [P, 2, 512], F32, r3 + 6 * K)
        rank = at("rank", [P, 3, 512], F32, r3 + 10 * K)
        selm = at("sel_mask", [P, 256 + 384 + 512], BF16, r5 + 8 * K)
        sqs = at("sq", [P, 2, 512], F32, rs + 4 * K)
        q_tok = at("q_tok", [P, NT, 512], F32, r1)
        k_tok = at("k_tok", [P, NT, 512], F32, r1 + 8 * K)
        qT = at("qT", [P, 4, SEQ], F32, r4)
        kT = at("kT", [P, 4, SEQ], F32, r4 + 8 * K)
        v_tok = at("v_tok", [P, NT, 512], F32, r5)
        tm = at("bias_masked", [P, 2, 512], F32, r1 + 8 * K)
        prob = at("prob", [P, 2, 512], F32, rs)
        probT = at("probT", [P, 2, 512], F32, rs + 4 * K)
        att_hi = at("att_hi", [P, 4, SEQ], F32R, r6)
        att_lo = at("att_lo", [P, 4, SEQ], F32R, r6 + 8 * K)
        xacc = at("xbc_acc", [P, 2, 512], F32)
        xbcT = at("xbcT", [P, 8, SEQ], F32, r3)
        z_tok = at("z_tok", [P, NT, 512], F32, r1)
        xs_tok = at("xs_tok", [P, NT, 512], F32, r1 + 8 * K)
        b_tok = at("b_tok", [P, 2, 256], F32, r5)
        state = at("state", [P, 512], F32, r5 + 2 * K)
        xd = at("xd", [P, 512], F32, r5 + 4 * K)
        xdd = at("xdd", [P, 512], F32, r5 + 6 * K)
        yb = at("yb", [P, 512], F32, r5 + 8 * K)
        xskip = xacc[:, 1, :]
        gssm = at("gssm", [P, 512], F32)
        dec = at("dec", [P, SH, P], F32, rs)
        sct = at("sct", [P, SH, P], F32, rs + 4 * K)
        ssm_hi = at("ssm_hi", [P, 4, SEQ], F32R, r4)
        ssm_lo = at("ssm_lo", [P, 4, SEQ], F32R, r4 + 8 * K)
        sig = at("sig", [P, 512], F32, rs)
        u_in = at("u_in", [P, 4, SEQ], F32, r7)
        u_acc = at("u_acc", [P, 4, SEQ], F32, r7 + 8 * K)
        u_tok = at("u_tok", [P, NT, 512], F32, r7)
        us = at("us", [P, 2, 512], F32, rs)
        conv_hi = at("conv_hi", [P, 4, SEQ], F32R, r2)
        conv_lo = at("conv_lo", [P, 4, SEQ], F32R, r2 + 8 * K)
        x2 = at("x2", [P, NT, DM], F32, r1)
        x2n = at("x2n", [P, NT, DM], F32, mix0)
        ghi = at("g_hi", [P, NF, SEQ], F32R, mix0)
        glo = at("g_lo", [P, NF, SEQ], F32R, mix0 + NF * SEQ * 4)
        ffn = mix0 + 2 * NF * SEQ * 4
        fbuf = at("f", [P, 4, SEQ], F32, ffn)
        sg = at("sg", [P, 2, SEQ], F32, ffn + 8 * K)
        gg = at("gg", [P, 2, SEQ], F32, ffn + 12 * K)
        y_out = at("y_out", [P, 8, 512], F32, ffn)
        assert max(top[0], ffn + 16 * K) <= nc.sbuf_usable_end
        MIX = {"att": (att_hi, att_lo), "conv": (conv_hi, conv_lo), "ssm": (ssm_hi, ssm_lo)}

        free = [0]

        def col(n):
            free[0] += n
            return st[:, free[0] - n:free[0]]

        ssq, rstd = col(NT), col(NT)
        half_neg = col(32)
        iwdt = col(NT * 12).rearrange("p (t c) -> p t c", c=12)
        hbc = col(3 * SH).rearrange("p (w h) -> p w h", h=SH)
        aneg = col(SH)
        dtx, dte, dtu, dtl, dtv, dta = (col(32) for _ in range(6))
        m8 = col(8)
        ssqk, rqk = col(64), col(64)
        mn, psum_p, rp = col(NT * NH), col(NT * NH), col(NT * NH)
        csx, ecs = col(96), col(96)
        yss, yrs = col(NT), col(NT)
        bn6 = col(6)
        mv = col(2 * NT).rearrange("p (t c) -> p t c", c=2)
        lnr = col(NT)
        ssq2, rstd2 = col(NT), col(NT)
        assert free[0] <= 816

        bank = [ctx.enter_context(nc.psum_tensor(f"bank{b}", [P, 512], F32)) for b in range(8)]

        def sem(name):
            return ctx.enter_context(nc.semaphore(name))

        s_x = [sem(f"x_landed{t}") for t in range(NT)]
        s_const, s_rows, s_small, s_hbc, s_oneh = (
            sem(n) for n in ("consts_made", "rows_landed", "small_landed",
                             "head_params_landed", "onehot_landed"))
        s_gout, s_trev, s_x2, s_yout = (
            sem(n) for n in ("gtable_stored", "trev_landed", "x2_landed", "y_stored"))
        w_landed = [sem(f"w_landed{n}") for n in range(NSLOT)]
        w_hi_ready, w_lo_ready = sem("w_hi_ready"), sem("w_lo_ready")
        ws_hi_ready, ws_lo_ready = sem("ws_hi_ready"), sem("ws_lo_ready")
        acc_step, aux_done, out_done = sem("acc_step"), sem("aux_done"), sem("out_done")
        drained = [sem(f"drained{b}") for b in range(8)]
        dve_step, act_step, pool_step = sem("dve_step"), sem("act_step"), sem("pool_step")
        hi_evac = sem("hi_evac")
        ssq_ready, ms_ready, rstd_ready = sem("ssq_ready"), sem("ms_ready"), sem("rstd_ready")
        xn_ready = sem("xn_ready")
        sig_ready, glu_ready = sem("sig_ready"), sem("glu_ready")
        relu_ready, relu_used, sel_ready = sem("relu_ready"), sem("relu_used"), sem("sel_ready")
        sq_ready, sq_used, qkms_ready, rqk_ready, qkn_ready = (
            sem(n) for n in ("sq_ready", "sq_used", "qkms_ready", "rqk_ready", "qkn_ready"))
        tm_ready, exp_ready, prob_ready = sem("tm_ready"), sem("exp_ready"), sem("prob_ready")
        nx_ready, dte_ready, dtu_ready, dtl_ready, dta_ready = (
            sem(n) for n in ("nx_ready", "dte_ready", "dtu_ready", "dtl_ready", "dta_ready"))
        xacc_ready, xconv_ready, xbc_ready = sem("xacc_ready"), sem("xconv_ready"), sem("xbc_ready")
        csx_ready, ecs_ready = sem("csx_ready"), sem("ecs_ready")
        seg_ready, dec_ready, sct_ready = sem("seg_ready"), sem("dec_ready"), sem("sct_ready")
        xd_ready = sem("xd_ready")
        yg_ready, yss_ready, yms_ready, yrs_ready, yn_ready = (
            sem(n) for n in ("yg_ready", "yss_ready", "yms_ready", "yrs_ready", "yn_ready"))
        state_ready = sem("state_ready")
        dw_ready, lnv_ready, lnr_ready, utok_ready = (
            sem(n) for n in ("dw_ready", "lnv_ready", "lnr_ready", "utok_ready"))
        us_ready, chi_ready, clo_ready = sem("us_ready"), sem("chi_ready"), sem("clo_ready")
        ssq2_ready, ms2_ready, rstd2_ready, x2n_ready = (
            sem(n) for n in ("ssq2_ready", "ms2_ready", "rstd2_ready", "x2n_ready"))
        f_ready, ftap_ready, sg_ready, gg_ready, ghi_ready, glo_ready = (
            sem(n) for n in ("f_ready", "ftap_ready", "sg_ready", "gg_ready", "ghi_ready",
                             "glo_ready"))
        y_ready = sem("y_ready")

        block = ctx.enter_context(nc.Block())

        def ps(*key):
            return bank[RING[key][2]]

        def finished(eng, *key):
            ring, n = RING[key][:2]
            if ring in ("acc", "out"):
                eng.wait_ge(acc_step if ring == "acc" else out_done, STEP[key])
            else:
                eng.wait_ge(aux_done, n + 1)

        def evacuated(eng, *key):
            eng.wait_ge(drained[RING[key][2]], RING[key][3] + 1)

        def drain(ins, *key):
            ins.then_inc(drained[RING[key][2]], 1)

        def claim(eng, *key):
            if RING[key][3]:
                eng.wait_ge(drained[RING[key][2]], RING[key][3])

        def before(key):
            same = [s for s in PLAN if s[0] == key[0]]
            return same.index(key)

        @block.sync
        def _(sp):
            def load(c):
                what, i = CHUNKS[c]
                if c >= NSLOT:
                    sp.wait_ge(w_lo_ready, c - NSLOT + 1)
                slot = wraw[:, c % NSLOT, :]
                done = w_landed[c % NSLOT]
                if what in ("iq", "xbc"):
                    c0 = C_IQ if what == "iq" else C_XBC + 256 * i
                    src = w_in[:, c0:c0 + 256].rearrange("(k p) n -> p k n", p=P)
                    dst = slot.rearrange("p (k n) -> p k n", k=KD)
                    for a in (0, 4):
                        sp.dma_start(dst[:, a:a + 4], src[:, a:a + 4]).then_inc(done, 16)
                elif what in ("conv", "up"):
                    w, ca, cg = (w_in, C_CA, C_CG) if what == "conv" else (w_up, 0, D_FF)
                    dst = slot.rearrange("p (k s n) -> p k s n", k=KD, s=2)
                    for s, c0 in enumerate((cg, ca)):
                        src = w[:, c0 + P * i:c0 + P * i + P].rearrange("(k p) n -> p k n", p=P)
                        sp.dma_start(dst[:, :, s], src).then_inc(done, 16)
                elif what == "down":
                    dst = slot.rearrange("p (k n) -> p k n", k=2)
                    for k in range(2):
                        r = P * (2 * i + k)
                        sp.dma_start(dst[:, k], w_down[r:r + P, :]).then_inc(done, 16)
                else:
                    if what == "out":
                        src = w_out[P * MIX_TILE[i[0]]:P * (MIX_TILE[i[0]] + 4),
                                    512 * i[1]:512 * i[1] + 512]
                    else:
                        c0 = {"q": C_Q, "k": C_K, "v": C_V, "z": C_Z}[what]
                        src = w_in[512 * i:512 * i + 512, c0:c0 + 512]
                    src = src.rearrange("(k p) n -> p k n", p=P)
                    dst = slot.rearrange("p (k n) -> p k n", k=4)
                    for a in (0, 2):
                        sp.dma_start(dst[:, a:a + 2], src[:, a:a + 2]).then_inc(done, 16)

            for t in range(NT):
                sp.dma_start(x_sb[:, t, :], x[P * t:P * t + P, :]).then_inc(s_x[t], 16)

            def put_rows(r, v):
                sp.dma_start(rows[r % P:r % P + v.shape[0], r // P, :], v).then_inc(s_rows, 16)

            def vec(v):
                return v.rearrange("o (r c) -> (o r) c", c=P)

            put_rows(R_GM, vec(norm_mix_g))
            put_rows(R_GF, vec(norm_ffn_g))
            put_rows(R_CB, vec(conv_dw_b))
            put_rows(R_LG, vec(conv_ln_g))
            put_rows(R_LB, vec(conv_ln_b))
            put_rows(R_SW, ssm_conv_w[0].rearrange("k (r c) -> (k r) c", c=P))
            put_rows(R_SB, vec(ssm_conv_b))
            put_rows(R_FB, vec(ffn_conv_b))
            for r, v in ((R_QG, q_norm_g), (R_KG, k_norm_g)):
                for s in range(2):
                    sp.dma_start(rows[r:r + 1, 0, HD * s:HD * s + HD], v).then_inc(s_rows, 16)
            put_rows(P, conv_dw_w[0].rearrange("k (r c) -> (k r) c", c=P))
            fw = ffn_conv_w[0].rearrange("k (r c) -> (k r) c", c=P)
            put_rows(2 * P, fw[0:P])
            put_rows(3 * P, fw[P:FK * 2 * NF])
            load(0)
            wsrc = w_in.rearrange("(k p) n -> p k n", p=P)
            for c0, n, at_ in ((C_IK, ID, 0), (C_IK, ID, ID), (C_IW, NIH, 128), (C_DT, SH, 132)):
                sp.dma_start(ws_raw[:, :, at_:at_ + n], wsrc[:, :, c0:c0 + n]).then_inc(s_small, 16)
            for w, v in enumerate((dt_bias, a_log, d_skip)):
                sp.dma_start(hbc[:, w, :], v.to_broadcast([P, SH])).then_inc(s_hbc, 16)
            sp.dma_start(gssm[:, :], ssm_norm_g.to_broadcast([P, 512])).then_inc(s_hbc, 16)
            sp.dma_start(oneh[:, :], onehot).then_inc(s_oneh, 16)
            sp.dma_start(relb[:, :], rel_bias).then_inc(s_oneh, 16)
            load(1)
            for s in PLAN:
                if s[0] == "split" and s[1] + NSLOT < UP0 + 2:
                    load(s[1] + 1) if s[1] == 1 else None
                    load(s[1] + NSLOT)
                elif s[0] == "gtab":
                    evacuated(sp, "gt", 0)
                    evacuated(sp, "gt", 1)
                    sp.dma_start(gdram, gsb[:, :]).then_inc(s_gout, 16)
                    sp.wait_ge(s_gout, 16)
                    finished(sp, "hT", KD - 1)
                    src = bass.AP(gdram.tensor, 0, [[1, P], [NG, NH], [1, 512]])
                    sp.dma_start(trev[:, :, :], src).then_inc(s_trev, 16)
                elif s == ("ssdT", NT - 1):
                    sp.wait_ge(yg_ready, NT)
                    sp.wait_ge(xd_ready, 3 * NT)
                    for t in range(NT):
                        sp.dma_start(x2[:, t, :], x[P * t:P * t + P, :]).then_inc(s_x2, 16)

            with sp.Fori(0, NF // 2 - 1) as n:
                for s in range(2):
                    c = UP0 + 2 + s
                    sp.wait_ge(w_lo_ready, n * 2 + (c - NSLOT + 1))
                    dst = wraw[:, c % NSLOT, :].rearrange("p (k s n) -> p k s n", k=KD, s=2)
                    for v, c0 in enumerate((D_FF, 0)):
                        src = w_up[:, bass.ds(n * (2 * P) + (c0 + P * (2 + s)), P)]
                        sp.dma_start(dst[:, :, v], src.rearrange("(k p) n -> p k n", p=P))\
                            .then_inc(w_landed[c % NSLOT], 16)
            for c in range(DN0, len(CHUNKS)):
                load(c)
            for t in range(NT):
                for half in range(2):
                    sp.wait_ge(y_ready, 2 * t + half + 1)
                    sp.dma_start(out[P * t:P * t + P, 512 * half:512 * half + 512],
                                 y_out[:, 2 * t + half, :]).then_inc(s_yout, 16)
            sp.wait_ge(s_yout, 16 * 2 * NT)

        @block.gpsimd
        def _(pool):
            n_link = [0]

            def link(ins):
                n_link[0] += 1
                ins.then_inc(pool_step, 1)
                pool.wait_ge(pool_step, n_link[0])

            link(pool.memset(ident[:, :], 0.0))
            link(pool.affine_select(out=ident[:, :], in_=ident[:, :], compare_op=ALU.not_equal,
                                    fill=1.0, base=0, pattern=[[-1, P]], channel_multiplier=1))
            link(pool.memset(half_neg, -0.5))
            link(pool.memset(ones[:, :], 1.0))
            link(pool.affine_select(out=tri[:, :], in_=ones[:, :], compare_op=ALU.is_ge, fill=0.0,
                                    base=0, pattern=[[1, P]], channel_multiplier=-1))
            link(pool.memset(neg_l[:, :], 0.0))
            link(pool.memset(jrev[:, :], 0.0))
            link(pool.affine_select(out=neg_q[:, :], in_=neg_l[:, :], compare_op=ALU.is_ge,
                                    fill=MASKED, base=0, pattern=[[-1, P]], channel_multiplier=1))
            link(pool.affine_select(out=neg_l[:, :], in_=neg_l[:, :], compare_op=ALU.is_ge,
                                    fill=MASKED, base=0, pattern=[[1, P]], channel_multiplier=-1))
            pool.affine_select(out=jrev[:, :], in_=jrev[:, :], compare_op=ALU.not_equal, fill=1.0,
                               base=-(P - 1), pattern=[[1, P]], channel_multiplier=1)\
                .then_inc(s_const, 1)

            def inverse_root(out_, in_, ready):
                n = out_.free_size()
                pool.tensor_tensor(out_, in_, half_neg[:, 0:n], ALU.pow).then_inc(ready, 1)

            for s in PLAN:
                k = s[0]
                if k == "norm1":
                    pool.wait_ge(ms_ready, 1)
                    inverse_root(rstd, ssq, rstd_ready)
                elif k == "qkev":
                    which = "qk".index(s[1])
                    pool.wait_ge(qkms_ready, before(s) + 1)
                    inverse_root(rqk[:, 32 * which:32 * which + 32],
                                 ssqk[:, 32 * which:32 * which + 32], rqk_ready)
                elif k == "score":
                    _, i, b, h = s
                    W = P * (b + 1)
                    if i == 0:
                        finished(pool, "qkT", "k", 3)
                        for hh in range(NH):
                            evacuated(pool, "tbias", hh)
                    if i >= 2:
                        evacuated(pool, "score", i - 2, *divmod(i - 2, NH))
                    if b:
                        pool.wait_ge(sel_ready, b)
                    m = neg_q[:, :] if b == 0 else selm[:, SEL0[b]:SEL0[b] + W]
                    pool.tensor_tensor(tm[:, i % 2, 0:W], tbias[:, h, 384 - P * b:384 - P * b + W],
                                       m, ALU.add).then_inc(tm_ready, 1)
                elif k == "ssd":
                    t = s[1]
                    if t == 0:
                        finished(pool, "pv", NT - 1)
                        pool.wait_ge(dta_ready, 1)
                        pool.wait_ge(s_hbc, 64)
                        for tt in range(NT):
                            evacuated(pool, "xs", tt)
                        pool.wait_ge(ecs_ready, 1)
                    else:
                        finished(pool, "yd", t - 1)
                        finished(pool, "st", t - 1)
                        pool.wait_ge(yg_ready, t)
                    v3 = xs_tok[:, t, :].rearrange("p (h c) -> p h c", h=SH)
                    x3, xx3, sk3 = (b_.rearrange("p (h c) -> p h c", h=SH)
                                    for b_ in (xd[:, :], xdd[:, :], xskip))

                    def per_head(ap):
                        return ap.unsqueeze(2).to_broadcast([P, SH, SP_])

                    pool.tensor_tensor(x3, v3, per_head(dtv[:, SH * t:SH * t + SH]), ALU.mult)\
                        .then_inc(xd_ready, 1)
                    pool.tensor_tensor(sk3, v3, per_head(hbc[:, 2, :]), ALU.mult)\
                        .then_inc(xd_ready, 1)
                    pool.wait_ge(xd_ready, 3 * t + 1)
                    pool.tensor_tensor(xx3, x3, per_head(ecs[:, 64 + SH * t:64 + SH * t + SH]),
                                       ALU.mult).then_inc(xd_ready, 1)
                elif k == "ssdT":
                    pool.wait_ge(yms_ready, s[1] + 1)
                    inverse_root(yrs[:, s[1]:s[1] + 1], yss[:, s[1]:s[1] + 1], yrs_ready)
                elif k == "ln":
                    pool.wait_ge(lnv_ready, s[1] + 1)
                    inverse_root(lnr[:, s[1]:s[1] + 1], mv[:, s[1], 1:2], lnr_ready)
            for t in range(NT):
                pool.wait_ge(ms2_ready, t + 1)
                inverse_root(rstd2[:, t:t + 1], ssq2[:, t:t + 1], rstd2_ready)

        @block.scalar
        def _(act):
            n_link = [0]

            def link(ins):
                n_link[0] += 1
                ins.then_inc(act_step, 1)
                act.wait_ge(act_step, n_link[0])

            n_hi = [0]

            def high(out_, in_, scale=1.0):
                n_hi[0] += 1
                act.activation(out_, in_, ACT.Copy, scale=scale).then_inc(hi_evac, 1)

            def split_hi(c):
                act.wait_ge(w_landed[c % NSLOT], 32 * (c // NSLOT + 1))
                if c >= NSLOT:
                    act.wait_ge(acc_step, STEP[("chunk", c - NSLOT)])
                act.activation(whi[:, c % NSLOT, :], wraw[:, c % NSLOT, :], ACT.Copy)\
                    .then_inc(w_hi_ready, 1)

            def conv_xbc(m):
                finished(act, "xbc", m)
                if m >= 2:
                    act.wait_ge(xbc_ready, m - 1)
                act.activation(xacc[:, m % 2, :], ps("xbc", m)[:, :], ACT.Identity,
                               bias=prm[:, R_SB + m:R_SB + m + 1],
                               scale=prm[:, R_SW + 24 + m:R_SW + 25 + m]).then_inc(xacc_ready, 1)

            def silu_xbc(m):
                evacuated(act, "xbc", m)
                act.activation(xbcT[:, m, :], xacc[:, m % 2, :], ACT.Silu).then_inc(xbc_ready, 1)

            for s in PLAN:
                k = s[0]
                if k == "prm":
                    finished(act, *s)
                    drain(act.activation(prm[:, :], ps(*s)[:, 0:N_PRM], ACT.Copy), *s)
                elif k == "norm1":
                    for t in range(NT):
                        act.wait_ge(s_x[t], 16)
                        act.activation(xn[:, t, :], x_sb[:, t, :], ACT.Square,
                                       accum_out=ssq[:, t:t + 1]).then_inc(ssq_ready, 1)
                elif k == "hT":
                    finished(act, *s)
                    evacuated(act, "prm")
                    high(hhi[:, s[1], :], ps(*s)[:, :], prm[:, R_GM + s[1]:R_GM + s[1] + 1])
                elif k == "small":
                    act.wait_ge(s_small, 64)
                    act.activation(ws_hi[:, :, :], ws_raw[:, :, :], ACT.Copy).then_inc(ws_hi_ready, 1)
                    split_hi(0)
                    finished(act, "ik")
                    drain(act.activation(ikT[:, :], ps("ik")[:, :], ACT.Copy), "ik")
                elif k == "dtprep":
                    act.wait_ge(nx_ready, 1)
                    act.activation(dte, dte, ACT.Exp).then_inc(dte_ready, 1)
                    act.wait_ge(s_hbc, 64)
                    act.activation(aneg, hbc[:, 1, :], ACT.Exp).then_inc(dte_ready, 1)
                    act.wait_ge(dtu_ready, 1)
                    act.activation(dtl, dtu, ACT.Ln).then_inc(dtl_ready, 1)
                elif k == "gtab":
                    for i in range(2):
                        finished(act, "gt", i)
                        n = 512 if i == 0 else NG - 512
                        drain(act.activation(gsb[:, 512 * i:512 * i + n], ps("gt", i)[0:NH, 0:n],
                                             ACT.Copy), "gt", i)
                elif k == "split":
                    split_hi(s[1])
                elif k == "mm" and CHUNKS[s[1]][0] == "iq":
                    for i in range(2):
                        finished(act, "iq", i)
                        drain(act.activation(iqT[:, i, :], ps("iq", i)[:, :], ACT.Copy), "iq", i)
                elif k == "glu":
                    j = s[1]
                    finished(act, "cg", j)
                    if j:
                        evacuated(act, "ca", j - 1)
                    drain(act.activation(sig[:, :], ps("cg", j)[:, :], ACT.Sigmoid), "cg", j)
                elif k == "tbias":
                    finished(act, *s)
                    drain(act.activation(tbias[:, s[1], :], ps(*s)[:, :], ACT.Copy), *s)
                elif k == "idx":
                    _, b, h = s
                    i = (b - 1) * NIH + h
                    W = P * (b + 1)
                    finished(act, *s)
                    if i >= 2:
                        act.wait_ge(relu_used, i - 1)
                    act.activation(relu[:, i % 2, 0:W], ps(*s)[:, 0:W], ACT.Relu,
                                   scale=ID ** -0.5 * NIH ** -0.5)\
                        .then_inc(drained[RING[s][2]], 1)
                elif k == "qkev":
                    tok = q_tok if s[1] == "q" else k_tok
                    for t in range(NT):
                        i = NT * before(s) + t
                        finished(act, s[1], t)
                        link(act.activation(tok[:, t, :], ps(s[1], t)[:, :], ACT.Copy))
                        if i >= 2:
                            act.wait_ge(sq_used, i - 1)
                        act.activation(sqs[:, i % 2, :], ps(s[1], t)[:, :], ACT.Square)\
                            .then_inc(drained[RING[(s[1], t)][2]], 1)
                elif k == "qkT":
                    dst, g = (qT, R_QG) if s[1] == "q" else (kT, R_KG)
                    for j in range(4):
                        key = ("qkT", s[1], j)
                        finished(act, *key)
                        drain(act.activation(dst[:, j, :], ps(*key)[:, :], ACT.Copy,
                                             scale=prm[:, g:g + 1]), *key)
                elif k == "vev":
                    for t in range(NT):
                        finished(act, "v", t)
                        drain(act.activation(v_tok[:, t, :], ps("v", t)[:, :], ACT.Copy), "v", t)
                elif k == "xbc":
                    conv_xbc(2 * s[1])
                    conv_xbc(2 * s[1] + 1)
                    silu_xbc(2 * s[1])
                    silu_xbc(2 * s[1] + 1)
                elif k == "zev":
                    for t in range(NT):
                        finished(act, "z", t)
                        drain(act.activation(z_tok[:, t, :], ps("z", t)[:, :], ACT.Silu), "z", t)
                elif k == "score":
                    _, i, b, h = s
                    evacuated(act, *s)
                    p = prob[:, i % 2, 0:P * (b + 1)]
                    act.activation(p, p, ACT.Exp, bias=mn[:, i:i + 1], scale=-1.0,
                                   accum_out=psum_p[:, i:i + 1]).then_inc(exp_ready, 1)
                elif k == "turn":
                    _, i, b, h = s
                    finished(act, *s)
                    if i >= 2:
                        act.wait_ge(out_done, i - 1)
                    W = P * (b + 1)
                    drain(act.activation(probT[:, i % 2, 0:W], ps(*s)[:, 0:W], ACT.Copy), *s)
                elif k == "attout":
                    b = s[1]
                    finished(act, "pv", b)
                    high(att_hi[:, :, P * b:P * b + P],
                         ps("pv", b)[:, :].rearrange("p (j q) -> p j q", j=4))
                elif k == "xt":
                    finished(act, "xs", s[1])
                    drain(act.activation(xs_tok[:, s[1], :], ps("xs", s[1])[:, :], ACT.Copy),
                          "xs", s[1])
                elif k == "cs":
                    act.wait_ge(csx_ready, 1)
                    act.activation(ecs, csx, ACT.Exp).then_inc(ecs_ready, 1)
                elif k == "ssd":
                    t = s[1]
                    for g in range(SG):
                        act.wait_ge(seg_ready, SG * t + g + 1)
                        d = dec[:, 4 * g:4 * g + 4, :]
                        act.activation(d, d, ACT.Exp).then_inc(dec_ready, 1)
                    if t < NT - 1:
                        finished(act, "bt", t)
                        drain(act.activation(b_tok[:, t % 2, :], ps("bt", t)[:, 0:256], ACT.Copy),
                              "bt", t)
                elif k == "ssdT":
                    t = s[1]
                    act.wait_ge(yg_ready, t + 1)
                    act.activation(xacc[:, 0, :], yb[:, :], ACT.Square,
                                   accum_out=yss[:, t:t + 1]).then_inc(yss_ready, 1)
                    finished(act, "yT", t)
                    high(ssm_hi[:, :, P * t:P * t + P],
                         ps("yT", t)[:, :].rearrange("p (j q) -> p j q", j=4))
                elif k == "lnT":
                    j = s[1]
                    finished(act, *s)
                    if j >= 2:
                        act.wait_ge(clo_ready, j - 1)
                    drain(act.activation(us[:, j % 2, :], ps(*s)[:, :], ACT.Silu,
                                         bias=prm[:, R_LB + j:R_LB + j + 1],
                                         scale=prm[:, R_LG + j:R_LG + j + 1]), *s)
                    evacuated(act, *s)
                    act.activation(conv_hi[:, j, :], us[:, j % 2, :], ACT.Copy).then_inc(chi_ready, 1)

            for t in range(NT):
                evacuated(act, "wo", "ssm", 1, t)
                act.activation(x2n[:, t, :], x2[:, t, :], ACT.Square,
                               accum_out=ssq2[:, t:t + 1]).then_inc(ssq2_ready, 1)
            for kk in range(KD):
                finished(act, "h2T", kk)
                high(hhi[:, kk, :], ps("h2T", kk)[:, :], prm[:, R_GF + kk:R_GF + kk + 1])

            with act.Fori(0, NF // 2) as n:
                for s in range(2):
                    c = UP0 + s + 1
                    act.wait_ge(w_landed[c % NSLOT], n * 32 + 32 * (c // NSLOT + 1))
                    if s == 0:
                        act.wait_ge(acc_step, n * 4 + STEP0)
                    else:
                        act.wait_ge(acc_step, n * 4 + STEP0 + 2)
                    act.activation(whi[:, c % NSLOT, :], wraw[:, c % NSLOT, :], ACT.Copy)\
                        .then_inc(w_hi_ready, 1)
                    act.wait_ge(gg_ready, n * 2 + (s + 1))
                    for v in range(2):
                        act.wait_ge(acc_step, n * 4 + STEP0 + 2 * s + v + 1)
                        tile = n * 2 + (s + (NF if v == 0 else 0))
                        act.activation(fbuf[:, 2 * s + v, :], bank[2 * s + v][:, :], ACT.Identity,
                                       bias=prm[:, bass.ds(tile + R_FB, 1)],
                                       scale=prm[:, bass.ds(tile + (R_FW + 2 * 2 * NF), 1)])\
                            .then_inc(f_ready, 1)
                    act.wait_ge(drained[2 * s], n + (ROUND0 + 1))
                    act.activation(sg[:, s, :], fbuf[:, 2 * s, :], ACT.Silu).then_inc(sg_ready, 1)
                    act.wait_ge(gg_ready, n * 2 + (s + 2))
                    act.activation(ghi[:, bass.ds(n * 2 + s, 1), :],
                                   gg[:, s:s + 1, :], ACT.Copy).then_inc(ghi_ready, 1)
            for c in range(DN0 + 1, len(CHUNKS)):
                split_hi(c)

        @block.vector
        def _(dve):
            n_link = [0]

            def link(ins):
                n_link[0] += 1
                ins.then_inc(dve_step, 1)
                dve.wait_ge(dve_step, n_link[0])

            def split_lo(c):
                dve.wait_ge(w_hi_ready, c + 1)
                slot = c % NSLOT
                dve.tensor_tensor(wlo[:, slot, :], wraw[:, slot, :], whi[:, slot, :].bitcast(F32),
                                  ALU.subtract).then_inc(w_lo_ready, 1)

            def wait_high(key):
                dve.wait_ge(hi_evac, HIGH.index(key) + 1)

            for s in PLAN:
                k = s[0]
                if k == "norm1":
                    dve.wait_ge(ssq_ready, NT)
                    dve.tensor_scalar(ssq, ssq, 1.0 / DM, EPS, ALU.mult, ALU.add).then_inc(ms_ready, 1)
                    dve.wait_ge(rstd_ready, 1)
                    for t in range(NT):
                        dve.tensor_scalar(xn[:, t, :], x_sb[:, t, :], rstd[:, t:t + 1], None,
                                          ALU.mult).then_inc(xn_ready, 1)
                elif k == "hT":
                    kk = s[1]
                    wait_high(s)
                    drain(dve.scalar_tensor_tensor(
                        out=hlo[:, kk, :], in0=ps(*s)[:, :], scalar=prm[:, R_GM + kk:R_GM + kk + 1],
                        in1=hhi[:, kk, :].bitcast(F32), op0=ALU.mult, op1=ALU.subtract), *s)
                elif k == "small":
                    dve.wait_ge(ws_hi_ready, 1)
                    dve.tensor_tensor(ws_lo[:, :, :], ws_raw[:, :, :], ws_hi[:, :, :].bitcast(F32),
                                      ALU.subtract).then_inc(ws_lo_ready, 1)
                    split_lo(0)
                elif k == "dtprep":
                    finished(dve, "iwdt")
                    drain(dve.tensor_copy(iwdt, ps("iwdt")[:, 0:12 * NT]
                                          .rearrange("p (t c) -> p t c", c=12)), "iwdt")
                    evacuated(dve, "iwdt")
                    dve.wait_ge(s_hbc, 64)
                    x3 = dtx.rearrange("p (t h) -> p t h", h=SH)
                    link(dve.tensor_tensor(x3, iwdt[:, :, NIH:],
                                           hbc[:, 0:1, :].to_broadcast([P, NT, SH]), ALU.add))
                    link(dve.tensor_scalar(dte, dtx, -1.0, None, ALU.mult))
                    dve.tensor_tensor(dte, dtx, dte, ALU.min).then_inc(nx_ready, 1)
                    dve.wait_ge(dte_ready, 1)
                    dve.tensor_scalar(dtu, dte, 1.0, None, ALU.add).then_inc(dtu_ready, 1)
                    dve.wait_ge(dtu_ready, 1)
                    dve.wait_ge(dtl_ready, 1)
                    link(dve.tensor_scalar(dta, dtu, -1.0, None, ALU.add))
                    link(dve.tensor_scalar(dtv, dta, 1e-30, None, ALU.max))
                    link(dve.reciprocal(dtv, dtv))
                    link(dve.tensor_tensor(dtv, dtv, dte, ALU.mult))
                    link(dve.tensor_tensor(dtv, dtv, dtl, ALU.mult))
                    link(dve.scalar_tensor_tensor(out=dta, in0=dta, scalar=0.0, in1=dte,
                                                  op0=ALU.is_equal, op1=ALU.mult))
                    link(dve.tensor_tensor(dtv, dtv, dta, ALU.add))
                    link(dve.scalar_tensor_tensor(out=dtv, in0=dtx, scalar=0.0, in1=dtv,
                                                  op0=ALU.max, op1=ALU.add))
                    dve.wait_ge(dte_ready, 2)
                    dve.scalar_tensor_tensor(
                        out=dta.rearrange("p (t h) -> p t h", h=SH),
                        in0=dtv.rearrange("p (t h) -> p t h", h=SH), scalar=-1.0,
                        in1=aneg.unsqueeze(1).to_broadcast([P, NT, SH]), op0=ALU.mult,
                        op1=ALU.mult).then_inc(dta_ready, 1)
                elif k == "split":
                    split_lo(s[1])
                elif k == "glu":
                    j = s[1]
                    finished(dve, "ca", j)
                    evacuated(dve, "cg", j)
                    drain(dve.tensor_tensor(u_in[:, j, :], ps("ca", j)[:, :], sig[:, :], ALU.mult),
                          "ca", j)
                elif k == "dw":
                    _, j, a, b = s
                    for i in range(a, b):
                        w = prm[:, R_CW + 4 * (CONV_K - 1 - i) + j:R_CW + 4 * (CONV_K - 1 - i) + j + 1]
                        if i == 0:
                            evacuated(dve, "ca", j)
                            link(dve.tensor_scalar(u_acc[:, j, :], u_in[:, j, :], w,
                                                   prm[:, R_CB + j:R_CB + j + 1], ALU.mult, ALU.add))
                            continue
                        ins = dve.scalar_tensor_tensor(
                            out=u_acc[:, j, i:], in0=u_in[:, j, 0:SEQ - i], scalar=w,
                            in1=u_acc[:, j, i:], op0=ALU.mult, op1=ALU.add)
                        if i == CONV_K - 1:
                            ins.then_inc(dw_ready, 1)
                        else:
                            link(ins)
                elif k == "idx":
                    _, b, h = s
                    i = (b - 1) * NIH + h
                    W = P * (b + 1)
                    evacuated(dve, *s)
                    r, iw = rank[:, b - 1, 0:W], iwdt[:, b, h:h + 1]
                    if h == 0:
                        dve.tensor_scalar(r, relu[:, i % 2, 0:W], iw, 0.0, ALU.mult, ALU.add)\
                            .then_inc(relu_used, 1)
                    else:
                        dve.wait_ge(relu_used, i)
                        dve.scalar_tensor_tensor(out=r, in0=relu[:, i % 2, 0:W], scalar=iw, in1=r,
                                                 op0=ALU.mult, op1=ALU.add).then_inc(relu_used, 1)
                    if h == NIH - 1:
                        dve.wait_ge(relu_used, i + 1)
                        d = rank[:, b - 1, W - P:W]
                        link(dve.tensor_tensor(d, d, neg_q[:, :], ALU.add))
                elif k == "topk":
                    _, b, r0, r1_ = s
                    r = rank[:, b - 1, 0:P * (b + 1)]
                    for _ in range(r0, r1_):
                        link(dve.max(m8, r))
                        link(dve.match_replace(r, m8, r, TAKEN))
                    if r1_ == TOPK // 8:
                        dve.tensor_scalar(selm[:, SEL0[b]:SEL0[b] + P * (b + 1)], r,
                                          0.5 * (MASKED + TAKEN), MASKED, ALU.is_gt, ALU.mult)\
                            .then_inc(sel_ready, 1)
                elif k == "qkev":
                    w = before(s)
                    for t in range(NT):
                        i = NT * w + t
                        evacuated(dve, s[1], t)
                        c = 32 * w + SH * t
                        dve.tensor_reduce(ssqk[:, c:c + NH],
                                          sqs[:, i % 2, :].rearrange("p (h c) -> p h c", h=NH),
                                          AX_X, ALU.add).then_inc(sq_used, 1)
                    dve.wait_ge(sq_used, NT * (w + 1))
                    a, b = (1.0, HD * EPS) if s[1] == "q" else (1.0 / HD, EPS)
                    c = ssqk[:, 32 * w:32 * w + 32]
                    dve.tensor_scalar(c, c, a, b, ALU.mult, ALU.add).then_inc(qkms_ready, 1)
                elif k == "qkn":
                    w = before(s)
                    tok = q_tok if s[1] == "q" else k_tok
                    dve.wait_ge(rqk_ready, w + 1)
                    for t in range(NT):
                        v3 = tok[:, t, :].rearrange("p (h c) -> p h c", h=NH)
                        c = 32 * w + NH * t
                        dve.tensor_tensor(v3, v3, rqk[:, c:c + NH].unsqueeze(2)
                                          .to_broadcast([P, NH, HD]), ALU.mult).then_inc(qkn_ready, 1)
                elif k == "score":
                    _, i, b, h = s
                    W = P * (b + 1)
                    finished(dve, *s)
                    dve.wait_ge(tm_ready, i + 1)
                    if i >= 2:
                        finished(dve, "turn", i - 2, *divmod(i - 2, NH))
                    dve.tensor_tensor_reduce(prob[:, i % 2, 0:W], ps(*s)[:, 0:W], tm[:, i % 2, 0:W],
                                             -1.0, 3.4e38, ALU.add, ALU.min, mn[:, i:i + 1])\
                        .then_inc(drained[RING[s][2]], 1)
                elif k == "turn":
                    _, i, b, h = s
                    dve.wait_ge(exp_ready, i + 1)
                    link(dve.reciprocal(rp[:, i:i + 1], psum_p[:, i:i + 1]))
                    p = prob[:, i % 2, 0:P * (b + 1)]
                    dve.tensor_scalar(p, p, rp[:, i:i + 1], None, ALU.mult).then_inc(prob_ready, 1)
                elif k == "attout":
                    b = s[1]
                    wait_high(s)
                    q = slice(P * b, P * b + P)
                    drain(dve.tensor_tensor(att_lo[:, :, q],
                                            ps("pv", b)[:, :].rearrange("p (j q) -> p j q", j=4),
                                            att_hi[:, :, q].bitcast(F32), ALU.subtract), "pv", b)
                elif k == "xbc":
                    for m in (2 * s[1], 2 * s[1] + 1):
                        dve.wait_ge(xacc_ready, m + 1)
                        for i in range(1, SK):
                            c = R_SW + 8 * (SK - 1 - i) + m
                            ins = dve.scalar_tensor_tensor(
                                out=xacc[:, m % 2, i:], in0=ps("xbc", m)[:, 0:SEQ - i],
                                scalar=prm[:, c:c + 1], in1=xacc[:, m % 2, i:], op0=ALU.mult,
                                op1=ALU.add)
                            if i < SK - 1:
                                link(ins)
                            else:
                                drain(ins, "xbc", m)
                elif k == "cs":
                    finished(dve, "cs")
                    drain(dve.tensor_copy(csx[:, 0:64], ps("cs")[:, 0:64]), "cs")
                    evacuated(dve, "cs")
                    dve.tensor_tensor(csx[:, 64:96], csx[:, 32:64], csx[:, 0:32], ALU.subtract)\
                        .then_inc(csx_ready, 1)
                elif k == "ssd":
                    t = s[1]
                    for g in range(SG):
                        d = dec[:, 4 * g:4 * g + 4, :]
                        finished(dve, "csr", t, g)
                        dve.wait_ge(csx_ready, 1)
                        if t:
                            evacuated(dve, "gt2", t - 1)
                        c = SH * t + 4 * g
                        drain(dve.tensor_tensor(
                            d, ps("csr", t, g)[:, :].rearrange("p (h l) -> p h l", h=4),
                            csx[:, c:c + 4].unsqueeze(2).to_broadcast([P, 4, P]), ALU.subtract),
                            "csr", t, g)
                        evacuated(dve, "csr", t, g)
                        dve.tensor_tensor(d, d, neg_l[:, :].unsqueeze(1).to_broadcast([P, 4, P]),
                                          ALU.add).then_inc(seg_ready, 1)
                    if t:
                        finished(dve, "yd", t - 1)
                    finished(dve, "gt2", t)
                    for g in range(SG):
                        dve.wait_ge(dec_ready, SG * t + g + 1)
                        ins = dve.tensor_tensor(
                            sct[:, 4 * g:4 * g + 4, :],
                            ps("gt2", t)[:, P * g:P * g + P].unsqueeze(1).to_broadcast([P, 4, P]),
                            dec[:, 4 * g:4 * g + 4, :], ALU.mult)
                        if g == SG - 1:
                            drain(ins, "gt2", t)
                elif k == "ssdout":
                    t = s[1]
                    y3 = yb[:, :].rearrange("p (h c) -> p h c", h=SH)
                    if t:
                        finished(dve, "yT", t - 1)
                        finished(dve, "yo", t)
                        drain(dve.tensor_tensor(
                            y3, ps("yo", t)[:, :].rearrange("p (h c) -> p h c", h=SH),
                            ecs[:, SH * t:SH * t + SH].unsqueeze(2).to_broadcast([P, SH, SP_]),
                            ALU.mult), "yo", t)
                        evacuated(dve, "yo", t)
                    finished(dve, "yd", t)
                    dve.wait_ge(xd_ready, 3 * t + 2)
                    other = yb[:, :] if t else xskip
                    drain(dve.tensor_tensor(yb[:, :], ps("yd", t)[:, :], other, ALU.add),
                          "yd", t)
                    evacuated(dve, "yd", t)
                    if t:
                        link(dve.tensor_tensor(yb[:, :], yb[:, :], xskip, ALU.add))
                    evacuated(dve, "z", t)
                    dve.tensor_tensor(yb[:, :], yb[:, :], z_tok[:, t, :], ALU.mult)\
                        .then_inc(yg_ready, 1)
                    if t < NT - 1:
                        s3 = state[:, :].rearrange("p (h c) -> p h c", h=SH)
                        if t:
                            c = 32 + SH * t
                            link(dve.tensor_tensor(s3, s3, ecs[:, c:c + SH].unsqueeze(2)
                                                   .to_broadcast([P, SH, SP_]), ALU.mult))
                        finished(dve, "st", t)
                        if t:
                            drain(dve.tensor_tensor(state[:, :], ps("st", t)[:, :], state[:, :],
                                                    ALU.add), "st", t)
                        else:
                            drain(dve.tensor_copy(state[:, :], ps("st", t)[:, :]), "st", t)
                elif k == "ssdT":
                    t = s[1]
                    dve.wait_ge(yss_ready, t + 1)
                    dve.tensor_scalar(yss[:, t:t + 1], yss[:, t:t + 1], 1.0 / 512, EPS, ALU.mult,
                                      ALU.add).then_inc(yms_ready, 1)
                    dve.wait_ge(yrs_ready, t + 1)
                    dve.scalar_tensor_tensor(out=yb[:, :], in0=yb[:, :], scalar=yrs[:, t:t + 1],
                                             in1=gssm[:, :], op0=ALU.mult, op1=ALU.mult)\
                        .then_inc(yn_ready, 1)
                    wait_high(s)
                    q = slice(P * t, P * t + P)
                    drain(dve.tensor_tensor(ssm_lo[:, :, q],
                                            ps("yT", t)[:, :].rearrange("p (j q) -> p j q", j=4),
                                            ssm_hi[:, :, q].bitcast(F32), ALU.subtract), "yT", t)
                elif k == "ln":
                    t = s[1]
                    finished(dve, *s)
                    link(dve.bn_stats(bn6, ps(*s)[:, :]))
                    link(dve.bn_aggr(mv[:, t, :], bn6))
                    dve.tensor_scalar(mv[:, t, 1:2], mv[:, t, 1:2], EPS, None, ALU.add)\
                        .then_inc(lnv_ready, 1)
                    dve.wait_ge(lnr_ready, t + 1)
                    dve.wait_ge(dw_ready, 4)
                    drain(dve.tensor_scalar(u_tok[:, t, :], ps(*s)[:, :], mv[:, t, 0:1],
                                            lnr[:, t:t + 1], ALU.subtract, ALU.mult), *s)
                elif k == "lnT":
                    j = s[1]
                    dve.wait_ge(chi_ready, j + 1)
                    dve.tensor_tensor(conv_lo[:, j, :], us[:, j % 2, :],
                                      conv_hi[:, j, :].bitcast(F32), ALU.subtract)\
                        .then_inc(clo_ready, 1)
                elif k == "mm" and CHUNKS[s[1]][0] == "out":
                    g, half = CHUNKS[s[1]][1]
                    order = ["att", "conv", "ssm"]
                    for t in range(NT):
                        finished(dve, "wo", g, half, t)
                        if g == "att":
                            dve.wait_ge(s_x2, 16 * NT)
                        else:
                            evacuated(dve, "wo", order[order.index(g) - 1], half, t)
                        xx = x2[:, t, 512 * half:512 * half + 512]
                        drain(dve.tensor_tensor(xx, ps("wo", g, half, t)[:, :], xx, ALU.add),
                              "wo", g, half, t)

            for t in range(NT):
                c = ssq2[:, t:t + 1]
                dve.wait_ge(ssq2_ready, t + 1)
                dve.tensor_scalar(c, c, 1.0 / DM, EPS, ALU.mult, ALU.add).then_inc(ms2_ready, 1)
            for t in range(NT):
                dve.wait_ge(rstd2_ready, t + 1)
                dve.tensor_scalar(x2n[:, t, :], x2[:, t, :], rstd2[:, t:t + 1], None, ALU.mult)\
                    .then_inc(x2n_ready, 1)
            for kk in range(KD):
                dve.wait_ge(hi_evac, len(HIGH) + kk + 1)
                drain(dve.scalar_tensor_tensor(
                    out=hlo[:, kk, :], in0=ps("h2T", kk)[:, :],
                    scalar=prm[:, R_GF + kk:R_GF + kk + 1], in1=hhi[:, kk, :].bitcast(F32),
                    op0=ALU.mult, op1=ALU.subtract), "h2T", kk)

            dve.sem_inc(gg_ready, 1)
            dve.sem_inc(glo_ready, 1)
            with dve.Fori(0, NF // 2) as n:
                for s in range(2):
                    c = UP0 + s + 1
                    dve.wait_ge(w_hi_ready, n * 2 + (c + 1))
                    dve.tensor_tensor(wlo[:, c % NSLOT, :], wraw[:, c % NSLOT, :],
                                      whi[:, c % NSLOT, :].bitcast(F32), ALU.subtract)\
                        .then_inc(w_lo_ready, 1)
                    for v in range(2):
                        dve.wait_ge(f_ready, n * 4 + (2 * s + v + 1))
                        tile = n * 2 + (s + (NF if v == 0 else 0))
                        for i in range(1, FK):
                            ins = dve.scalar_tensor_tensor(
                                out=fbuf[:, 2 * s + v, i:], in0=bank[2 * s + v][:, 0:SEQ - i],
                                scalar=prm[:, bass.ds(tile + (R_FW + 2 * NF * (FK - 1 - i)), 1)],
                                in1=fbuf[:, 2 * s + v, i:], op0=ALU.mult, op1=ALU.add)
                            if i == 1:
                                ins.then_inc(ftap_ready, 1)
                                dve.wait_ge(ftap_ready, n * 4 + (2 * s + v + 1))
                            else:
                                ins.then_inc(drained[2 * s + v], 1)
                    dve.wait_ge(sg_ready, n * 2 + (s + 1))
                    dve.wait_ge(drained[2 * s + 1], n + (ROUND0 + 1))
                    dve.wait_ge(glo_ready, n * 2 + (s + 1))
                    dve.tensor_tensor(gg[:, s, :], fbuf[:, 2 * s + 1, :], sg[:, s, :], ALU.mult)\
                        .then_inc(gg_ready, 1)
                    dve.wait_ge(ghi_ready, n * 2 + (s + 1))
                    jj = n * 2 + s
                    dve.tensor_tensor(glo[:, bass.ds(jj, 1), :], gg[:, s:s + 1, :],
                                      ghi[:, bass.ds(jj, 1), :].bitcast(F32), ALU.subtract)\
                        .then_inc(glo_ready, 1)
            for c in range(DN0 + 1, len(CHUNKS)):
                split_lo(c)
            for t in range(NT):
                for half in range(2):
                    i = 2 * t + half
                    dve.wait_ge(acc_step, STEP[("chunk", len(CHUNKS) - 2)] + i + 1)
                    dve.tensor_tensor(y_out[:, i, :], bank[i][:, :],
                                      x2[:, t, 512 * half:512 * half + 512], ALU.add)\
                        .then_inc(y_ready, 1)

        @block.tensor
        def _(pe):
            def passes(hi, lo):
                return ((hi[0], hi[1]), (hi[0], lo[1]), (lo[0], hi[1]))

            def product(o, terms, first=True, last=True):
                n = len(terms)
                for i, (whi_, wlo_, mhi, mlo) in enumerate(terms):
                    for q, (a, b) in enumerate(((whi_, mhi), (whi_, mlo), (wlo_, mhi))):
                        ins = pe.matmul(o, a, b, start=first and i == 0 and q == 0,
                                        stop=last and i == n - 1 and q == 2)
                return ins

            def turn(o, in_):
                n = in_.shape[0]
                return pe.transpose(o, in_, ident[0:n, 0:n])

            def channels(c, bank_of):
                sl = c % NSLOT
                h, l = (w[:, sl, :].rearrange("p (k s n) -> p k s n", k=KD, s=2) for w in (whi, wlo))
                for v in range(2):
                    o = bank_of(v)
                    product(o, [(h[:, kk, v], l[:, kk, v], hhi[:, kk, :], hlo[:, kk, :])
                                for kk in range(KD)]).then_inc(acc_step, 1)

            for s in PLAN:
                k = s[0]
                if k == "prm":
                    pe.wait_ge(s_const, 1)
                    pe.wait_ge(s_rows, 16 * 15)
                    c = 0
                    for i, n in enumerate((N_ROW0, 4 * CONV_K, P, FK * 2 * NF - P)):
                        ins = turn(ps(*s)[:, c:c + n], rows[0:n, i, :])
                        c += n
                    ins.then_inc(aux_done, 1)
                elif k == "hT":
                    pe.wait_ge(xn_ready, NT)
                    claim(pe, *s)
                    for t in range(NT):
                        ins = turn(ps(*s)[:, P * t:P * t + P], xn[:, t, P * s[1]:P * s[1] + P])
                    ins.then_inc(aux_done, 1)
                elif k == "small":
                    pe.wait_ge(ws_lo_ready, 1)
                    for kk in range(KD):
                        evacuated(pe, "hT", kk)
                    product(ps("ik")[:, :], [(ws_hi[:, kk, 0:P], ws_lo[:, kk, 0:P], hhi[:, kk, :],
                                              hlo[:, kk, :]) for kk in range(KD)])\
                        .then_inc(acc_step, 1)
                    for t in range(NT):
                        q = slice(P * t, P * t + P)
                        ins = product(ps("iwdt")[:, 12 * t:12 * t + 12],
                                      [(hhi[:, kk, q], hlo[:, kk, q], ws_hi[:, kk, P:],
                                        ws_lo[:, kk, P:]) for kk in range(KD)])
                    ins.then_inc(acc_step, 1)
                elif k == "gtab":
                    pe.wait_ge(s_oneh, 32)
                    for i in range(2):
                        claim(pe, "gt", i)
                        n = 512 if i == 0 else NG - 512
                        pe.matmul(ps("gt", i)[0:NH, 0:n], relb[:, :], oneh[:, 512 * i:512 * i + n],
                                  start=True, stop=True).then_inc(aux_done, 1)
                elif k == "mm":
                    c = s[1]
                    what, i = CHUNKS[c]
                    pe.wait_ge(w_lo_ready, c + 1)
                    if what in ("iq", "xbc", "conv"):
                        keys = [("cg", i), ("ca", i)] if what == "conv" else \
                            [(what, 2 * i), (what, 2 * i + 1)]

                        def claimed(v):
                            claim(pe, *keys[v])
                            return ps(*keys[v])[:, :]

                        channels(c, claimed)
                        continue
                    w_h, w_l = (w[:, c % NSLOT, :].rearrange("p (k n) -> p k n", k=4)
                                for w in (whi, wlo))
                    if what == "out":
                        g, half = i
                        m_h, m_l = MIX[g]
                        if half == 0:
                            if g == "att":
                                evacuated(pe, "pv", NT - 1)
                            elif g == "conv":
                                pe.wait_ge(clo_ready, 4)
                            else:
                                for t in range(NT):
                                    evacuated(pe, "yT", t)
                        k0 = 0
                    else:
                        m_h, m_l = hhi, hlo
                        k0 = 4 * i
                    for t in range(NT):
                        q = slice(P * t, P * t + P)
                        key = ("wo", g, half, t) if what == "out" else (what, t)
                        if what == "out" or i == 0:
                            claim(pe, *key)
                        ins = product(ps(*key)[:, :], [(m_h[:, k0 + kk, q], m_l[:, k0 + kk, q],
                                                        w_h[:, kk, :], w_l[:, kk, :])
                                                       for kk in range(4)],
                                      first=what == "out" or i == 0, last=what == "out" or i == 1)
                        if what == "out" or i == 1 or t == NT - 1:
                            ins.then_inc(acc_step, 1)
                elif k == "tbias":
                    pe.wait_ge(s_trev, 16)
                    claim(pe, *s)
                    pe.matmul(ps(*s)[:, :], jrev[:, :], trev[:, s[1], :], start=True, stop=True)\
                        .then_inc(aux_done, 1)
                elif k == "idx":
                    _, b, h = s
                    r = slice(ID * (h % 2), ID * (h % 2) + ID)
                    evacuated(pe, "ik")
                    evacuated(pe, "iq", h // 2)
                    claim(pe, *s)
                    pe.matmul(ps(*s)[:, 0:P * (b + 1)], iqT[r, h // 2, P * b:P * b + P],
                              ikT[r, 0:P * (b + 1)], start=True, stop=True).then_inc(aux_done, 1)
                elif k == "qkT":
                    tok = q_tok if s[1] == "q" else k_tok
                    pe.wait_ge(qkn_ready, NT * (before(s) + 1))
                    for j in range(4):
                        claim(pe, "qkT", s[1], j)
                        for t in range(NT):
                            ins = turn(ps("qkT", s[1], j)[:, P * t:P * t + P],
                                       tok[:, t, P * j:P * j + P])
                        ins.then_inc(aux_done, 1)
                elif k == "score":
                    _, i, b, h = s
                    r = slice(HD * (h % 2), HD * (h % 2) + HD)
                    evacuated(pe, "qkT", "q", h // 2)
                    evacuated(pe, "qkT", "k", h // 2)
                    claim(pe, *s)
                    pe.matmul(ps(*s)[:, 0:P * (b + 1)], qT[r, h // 2, P * b:P * b + P],
                              kT[r, h // 2, 0:P * (b + 1)], start=True, stop=True)\
                        .then_inc(aux_done, 1)
                elif k == "turn":
                    _, i, b, h = s
                    pe.wait_ge(prob_ready, i + 1)
                    claim(pe, *s)
                    for j in range(b + 1):
                        ins = turn(ps(*s)[:, P * j:P * j + P], prob[:, i % 2, P * j:P * j + P])
                    ins.then_inc(aux_done, 1)
                elif k == "pv":
                    _, i, b, h = s
                    evacuated(pe, "turn", i, b, h)
                    if h == 0:
                        claim(pe, "pv", b)
                        for t in range(NT):
                            evacuated(pe, "v", t)
                    r = slice(HD * (h % 2), HD * (h % 2) + HD)
                    for j in range(b + 1):
                        ins = pe.matmul(ps("pv", b)[r, P * (h // 2):P * (h // 2) + P],
                                        v_tok[:, j, HD * h:HD * h + HD],
                                        probT[:, i % 2, P * j:P * j + P], start=j == 0, stop=j == b)
                    ins.then_inc(out_done, 1)
                elif k == "xt":
                    t = s[1]
                    pe.wait_ge(xbc_ready, 8)
                    claim(pe, "xs", t)
                    for j in range(4):
                        ins = turn(ps("xs", t)[:, P * j:P * j + P], xbcT[:, j, P * t:P * t + P])
                    ins.then_inc(aux_done, 1)
                elif k == "cs":
                    pe.wait_ge(dta_ready, 1)
                    claim(pe, "cs")
                    pe.matmul(ps("cs")[:, 0:32], tri[:, :], dta, start=True, stop=True)
                    pe.matmul(ps("cs")[:, 32:64], ones[:, :], dta, start=True, stop=True)\
                        .then_inc(aux_done, 1)
                elif k == "ssd":
                    t = s[1]
                    q = slice(P * t, P * t + P)
                    for g in range(SG):
                        claim(pe, "csr", t, g)
                        for h in range(4):
                            c = SH * t + 4 * g + h
                            ins = pe.matmul(ps("csr", t, g)[:, P * h:P * h + P],
                                            dta[:, c:c + 1].to_broadcast([P, P]), tri[:, :],
                                            start=True, stop=True)
                        ins.then_inc(aux_done, 1)
                    claim(pe, "gt2", t)
                    for g in range(SG):
                        ins = pe.matmul(ps("gt2", t)[:, P * g:P * g + P], xbcT[:, 4 + g, q],
                                        xbcT[:, 6 + g, q], start=True, stop=True)
                    ins.then_inc(aux_done, 1)
                    if t < NT - 1:
                        claim(pe, "bt", t)
                        for g in range(SG):
                            ins = turn(ps("bt", t)[:, P * g:P * g + P], xbcT[:, 4 + g, q])
                        ins.then_inc(aux_done, 1)
                elif k == "ssdout":
                    t = s[1]
                    q = slice(P * t, P * t + P)
                    evacuated(pe, "gt2", t)
                    pe.wait_ge(xd_ready, 3 * t + 3)
                    claim(pe, "yd", t)
                    for h in range(SH):
                        c = slice(SP_ * h, SP_ * h + SP_)
                        ins = pe.matmul(ps("yd", t)[:, c], sct[:, h, :], xd[:, c], start=True,
                                        stop=True)
                    ins.then_inc(out_done, 1)
                    if t:
                        evacuated(pe, "st", t - 1)
                        claim(pe, "yo", t)
                        for g in range(SG):
                            c = slice(256 * g, 256 * g + 256)
                            ins = pe.matmul(ps("yo", t)[:, c], xbcT[:, 6 + g, q], state[:, c],
                                            start=True, stop=True)
                        ins.then_inc(aux_done, 1)
                    if t < NT - 1:
                        evacuated(pe, "bt", t)
                        claim(pe, "st", t)
                        for g in range(SG):
                            c = slice(256 * g, 256 * g + 256)
                            ins = pe.matmul(ps("st", t)[:, c], b_tok[:, t % 2, P * g:P * g + P],
                                            xdd[:, c], start=True, stop=True)
                        ins.then_inc(aux_done, 1)
                elif k == "ssdT":
                    t = s[1]
                    pe.wait_ge(yn_ready, t + 1)
                    claim(pe, "yT", t)
                    for j in range(4):
                        ins = turn(ps("yT", t)[:, P * j:P * j + P], yb[:, P * j:P * j + P])
                    ins.then_inc(aux_done, 1)
                elif k == "ln":
                    pe.wait_ge(dw_ready, 4)
                    claim(pe, *s)
                    for j in range(4):
                        ins = turn(ps(*s)[:, P * j:P * j + P], u_acc[:, j, P * s[1]:P * s[1] + P])
                    ins.then_inc(aux_done, 1)
                elif k == "lnT":
                    for t in range(NT):
                        evacuated(pe, "ln", t)
                    claim(pe, *s)
                    for t in range(NT):
                        ins = turn(ps(*s)[:, P * t:P * t + P], u_tok[:, t, P * s[1]:P * s[1] + P])
                    ins.then_inc(aux_done, 1)

            pe.wait_ge(x2n_ready, NT)
            for kk in range(KD):
                claim(pe, "h2T", kk)
                for t in range(NT):
                    ins = turn(ps("h2T", kk)[:, P * t:P * t + P], x2n[:, t, P * kk:P * kk + P])
                ins.then_inc(aux_done, 1)
            for kk in range(KD):
                evacuated(pe, "h2T", kk)

            with pe.Fori(0, NF // 2) as n:
                for s in range(2):
                    c = UP0 + s
                    pe.wait_ge(w_lo_ready, n * 2 + (c + 1))

                    def claimed(v):
                        pe.wait_ge(drained[2 * s + v], n + ROUND0)
                        return bank[2 * s + v][:, :]

                    channels(c, claimed)

            for b in range(8):
                pe.wait_ge(drained[b], DRAINS[b] + (NF // 2 if b < 4 else 0))
            for j in range(NF // 2):
                c = DN0 + j
                pe.wait_ge(w_lo_ready, c + 1)
                if j == 0:
                    pe.wait_ge(glo_ready, NF + 1)
                w_h, w_l = (w[:, c % NSLOT, :].rearrange("p (k n) -> p k n", k=2)
                            for w in (whi, wlo))
                for t in range(NT):
                    q = slice(P * t, P * t + P)
                    for half in range(2):
                        f = slice(512 * half, 512 * half + 512)
                        ins = product(bank[2 * t + half][:, :],
                                      [(ghi[:, 2 * j + kk, q], glo[:, 2 * j + kk, q],
                                        w_h[:, kk, f], w_l[:, kk, f]) for kk in range(2)],
                                      first=j == 0, last=j == NF // 2 - 1)
                        if j == NF // 2 - 1 or (t, half) == (NT - 1, 1):
                            ins.then_inc(acc_step, 1)


_INS = ["x", "rel_bias", "norm_mix_g", "w_in", "conv_dw_w", "conv_dw_b", "conv_ln_g", "conv_ln_b",
        "q_norm_g", "k_norm_g", "ssm_conv_w", "ssm_conv_b", "dt_bias", "a_log", "d_skip",
        "ssm_norm_g", "w_out", "norm_ffn_g", "w_up", "ffn_conv_w", "ffn_conv_b", "w_down"]


def kernel(**inputs):
    import concourse.bacc as bacc
    from concourse.bass_utils import run_bass_kernel_spmd

    nc = bacc.Bacc("TRN2", target_bir_lowering=False, num_devices=1)
    arrays = {f"in_{n}": np.ascontiguousarray(inputs[n]) for n in _INS}
    arrays["in_onehot"] = bucket_onehot()
    args = [nc.dram_tensor(n, a.shape, mybir.dt.from_np(a.dtype), kind="ExternalInput").ap()
            for n, a in arrays.items()]
    out = nc.dram_tensor("out_x", (1, SEQ, DM), F32, kind="ExternalOutput").ap()
    build(nc, *args, out)
    r = run_bass_kernel_spmd(nc, [arrays], core_ids=[0])
    return r.results[0]["out_x"]
```

```python
from contextlib import ExitStack

import numpy as np

import concourse.bass as bass
from concourse import mybir

ALU = mybir.AluOpType
ACT = mybir.ActivationFunctionType
AX_X = mybir.AxisListType.X
F32 = mybir.dt.float32
F32R = mybir.dt.float32r
BF16 = mybir.dt.bfloat16

P = 128
SEQ, DM = 512, 1024
NT = SEQ // P
KD = DM // P
EPS = 1e-6
CONV_CH, CONV_K = 512, 31
NH, HD = 8, 64
NIH, ID = 4, 64
TOPK = 128
NBUCKET, MAXDIST = 32, 128
SH, SP_, SG, SK = 8, 64, 2, 4
D_FF, FK = 2816, 3
NF = D_FF // P
COLS = np.cumsum([0, CONV_CH, CONV_CH, 512, 512, 512, NIH * ID, ID, NIH, 512, 1024, SH])
C_CA, C_CG, C_Q, C_K, C_V, C_IQ, C_IK, C_IW, C_Z, C_XBC, C_DT = [int(v) for v in COLS[:-1]]
MASKED = -3.0e38
TAKEN = -3.3e38
NG = 640

R_CB, R_LG, R_LB, R_SW, R_SB, R_FB = 0, 4, 8, 12, 44, 52
R_QG, R_KG = 96, 97
N_ROW0 = 98
R_CW = N_ROW0
R_FW = R_CW + CONV_K * 4
N_PRM = R_FW + FK * 2 * NF

MIX_TILE = {"att": 4, "conv": 0, "ssm": 8}
CHUNKS = [("iq", 0)]
for what in "qkv":
    CHUNKS += [(what, 0), (what, 1)]
CHUNKS += [("conv", j) for j in range(4)] + [("xbc", j) for j in range(4)] + [("z", 0), ("z", 1)]
CHUNKS += [("out", (g, half)) for g in MIX_TILE for half in range(2)]
UP0 = len(CHUNKS)
CHUNKS += [("up", j) for j in range(NF)]
DN0 = len(CHUNKS)
CHUNKS += [("down", j) for j in range(NF // 2)]
NSLOT = 2


def bucket_onehot():
    n = np.maximum(511 - np.arange(NG), 0)
    nf = np.maximum(n, 1).astype(np.float32)
    half = NBUCKET // 2
    large = half + (np.log(nf / np.float32(half)) / np.float32(np.log(MAXDIST / half))
                    * np.float32(NBUCKET - half)).astype(np.int32)
    b = np.where(n < half, n, np.minimum(large, NBUCKET - 1))
    return (np.arange(NBUCKET)[:, None] == b[None, :]).astype(np.float32)


TOP_SLOTS = (9, 34)
DW_SLOTS = (38, 49, 69)
SSD_SLOTS = (67, 71, 76, 80)
DW_POOL = 1
POOL_COLS = 640
POOL_LO = [c for c in range(UP0) if CHUNKS[c] not in (("k", 1), ("v", 1))]


def make_plan():
    slots = [[("mg", n // 4, n % 4)] for n in range(4 * UP0)]
    front = [[] for _ in slots]

    def put(n, *steps):
        slots[n] += steps

    fill = [[] for _ in slots]
    for c in range(1, UP0 + 1):
        fill[4 * c - 4].append(("hi", c))
        fill[4 * c - 3].append(("lo", c))

    def spread(steps, a, b):
        for i, st_ in enumerate(steps):
            fill[a + i * (b - a + 1) // len(steps)].append(st_)

    at = {c: 4 * n for n, c in enumerate(CHUNKS[:UP0])}

    put(2, ("ev", "iq", 0))
    put(3, ("small",), ("ev", "ik", 0), ("ev", "iq", 1))
    put(4, ("iwT",), ("dt", 0))
    put(6, ("dt", 1))
    put(8, ("dt", 2))
    for n, b in ((5, 1), (6, 2), (8, 3)):
        put(n, *[("idx", b, h) for h in range(NIH)])
    rounds = [(k, b, r) for r in range(TOPK // 8) for k in ("topmax", "topmark") for b in (1, 2, 3)]
    spread(rounds, *TOP_SLOTS)
    put(TOP_SLOTS[1] + 1, ("sel",))
    put(1, ("gtab",))
    for h in range(NH):
        put(11 + h, ("tbias", h))
    for w, what in enumerate("qk"):
        n = at[(what, 1)]
        for t in range(NT):
            put(n + 1 + t, ("qkev", what, t))
        fill[n + 4].append(("qkms", what))
        front[n + 7].append(("qkn", what))
        put(n + 8, ("qkT", what, 0), ("qkT", what, 1))
        put(n + 9, ("qkT", what, 2), ("qkT", what, 3))
    for t in range(NT):
        put(at[("v", 1)] + 1 + t, ("ev", "v", t))
    a0 = at[("v", 1)] + 4
    for i in range(NT * NH):
        b, h = divmod(i, NH)
        front[a0 + i] += [("share", i - 1)] * (i > 0) + [("evT", i - 2)] * (i > 1)
        front[a0 + i].append(("score", i, b, h))
        put(a0 + i + 1, ("turn", i, b, h))
        put(a0 + i + 2, ("pv", i, b, h))
        if h == NH - 1:
            front[a0 + i + 3].append(("attout", b))
    n = NT * NH
    front[a0 + n] += [("share", n - 1), ("evT", n - 2)]
    front[a0 + n + 1].append(("evT", n - 1))
    for j in range(4):
        n = at[("conv", j)]
        put(n + 2, ("ev", "cg", j))
        put(n + 4, ("ev", "ca", j))
    for n in (1, 3):
        fill[at[("conv", n)] + 5] += [("glu", n - 1), ("glu", n)]
    d0, d1, d2 = DW_SLOTS
    spread([("dw", 0, i) for i in range(CONV_K)], d0, d1)
    spread([("dwp", DW_POOL, i) for i in range(1, CONV_K)], d0, d2 - 5)
    spread([("dw", DW_POOL, i) for i in range(CONV_K)], d0 + 1, d2 - 4)
    spread([("dw", j, i) for i in range(CONV_K) for j in (2, 3)], d1 + 1, d2)
    for t in range(NT):
        put(d2 + 1 + t // 2, ("ln", t))
        front[d2 + 2 + t // 2].append(("lnn", t))
    for j in range(4):
        put(d2 + 4 + j // 2, ("lnT", j))
    for m in range(8):
        n = at[("xbc", 0)] + 2 * m + 2
        put(n, ("xbase", m))
        put(n + 1, *[("xtap", m, i) for i in range(1, SK)])
    s0 = at[("z", 0)] + 2
    put(s0, ("silux",), ("cs",))
    put(s0 + 1, *[("xt", t) for t in range(NT)])
    for t in range(NT):
        put(at[("z", 1)] + 1 + t, ("ev", "z", t))
    put(at[("z", 1)] + 5, ("siluz",))
    for t, n in enumerate(SSD_SLOTS):
        put(n, ("csr", t))
        front[n + 1].append(("seg", t))
        put(n + 1, ("ssd", t))
        front[n + 2].append(("sct", t))
        put(n + 2, ("yd", t))
        front[n + 3].append(("ssdout", t))
        put(n + 3, ("ysq", t))
        put(n + 4, ("yms", t))
        front[n + 5].append(("yn", t))
        put(n + 5, ("yT", t))
        front[n + 6].append(("ssdT", t))
    for t in range(NT):
        put(at[("out", ("ssm", 0))] + 2 + t, ("sq2", t, 0))
    for c in range(at[("out", ("att", 0))], 4 * UP0 - 1):
        (g, half), t = CHUNKS[c // 4][1], c % 4
        put(c + 1, ("wo", g, half, t))
    last = 4 * UP0 - 1
    for t in range(NT - 1):
        put(last - 3 + t + 1, ("sq2", t, 1))
        if t < NT - 2:
            front[last - 3 + t + 2].append(("norm2", t))
            put(last - 3 + t + 2, ("h2", t))
            if t < NT - 3:
                put(last - 3 + t + 3, ("h2ev", t))
    return [step for parts in zip(front, slots, fill) for part in parts for step in part] + [
        ("wo", "ssm", 1, NT - 1), ("sq2", NT - 1, 1), ("norm2", NT - 2), ("h2", NT - 2),
        ("h2ev", NT - 3), ("norm2", NT - 1), ("h2", NT - 1), ("h2ev", NT - 2), ("h2ev", NT - 1)]


PLAN = [("norm", t) for t in range(NT)] + [("hi", 0), ("lo", 0)]
PLAN += [("wsplit",), ("prm",)] + make_plan()


def make_groups():
    acc, aux, out, step = [], [], [], {}
    n = n_out = 0

    def group(*key):
        nonlocal n
        acc.append(key)
        n += 1
        step[key] = n

    for s in PLAN:
        k = s[0]
        if k in ("prm", "tbias", "idx", "score", "turn", "ln", "lnT", "qkT", "cs", "iwT",
                 "yT"):
            aux.append(s)
        elif k in ("norm", "h2"):
            aux += [("hT" if k == "norm" else "h2T", s[1], g) for g in range(2)]
        elif k == "small":
            aux.append(("ik", 0))
        elif k == "gtab":
            aux += [("gt", 0), ("gt", 1)]
        elif k == "pv":
            n_out += 1
            if s[3] == 0:
                out.append(("pv", s[2]))
            step[("pv", s[2])] = n_out
        elif k == "xt":
            aux.append(("xs", s[1]))
        elif k == "csr":
            aux += [("csr", s[1], 0), ("csr", s[1], 1)]
        elif k == "ssd":
            aux.append(("gt2", s[1]))
            if s[1] < NT - 1:
                aux.append(("bt", s[1]))
        elif k == "yd":
            out.append(("yd", s[1]))
            n_out += 1
            step[("yd", s[1])] = n_out
            if s[1] > 0:
                aux.append(("yo", s[1]))
            if s[1] < NT - 1:
                aux.append(("st", s[1]))
        elif k == "mg":
            _, c, q = s
            what, i = CHUNKS[c]
            if what in ("iq", "xbc", "conv"):
                key = ("cg" if q < 2 else "ca", i) if what == "conv" else (what, 2 * i + q // 2)
                if q % 2 == 0:
                    acc.append(key)
                else:
                    n += 1
                    step[key] = n
            elif what == "out":
                group("wo", *i, q)
            elif i == 0:
                acc.append((what, q))
                n += q == 3
            else:
                n += 1
                step[(what, q)] = n
            if q == 3:
                step[("chunk", c)] = n
    return acc, aux, out, step, n


ACC, AUX, OUT, STEP, STEP0 = make_groups()
for j in range(NF):
    STEP[("chunk", UP0 + j)] = STEP0 + 2 * (j + 1)
for j in range(NF // 2):
    STEP[("chunk", DN0 + j)] = STEP0 + 2 * NF + j + 1
SQ2 = [s for s in PLAN if s[0] == "sq2"]
HIGH = []
for s in PLAN:
    if s[0] == "norm":
        HIGH += [("hT", s[1], 0), ("hT", s[1], 1)]
    elif s[0] in ("attout", "ssdT"):
        HIGH.append(s)
    elif s[0] == "h2ev":
        HIGH += [("h2T", s[1], 0), ("h2T", s[1], 1)]
SEL0 = {1: 0, 2: 256, 3: 640}
FFN_BANK = [(len(ACC) + i) % 4 for i in range(4)]
ROUND0 = [(len(ACC) + i) // 4 for i in range(4)]
RING = {}
for ring, groups, first, count in (("acc", ACC, 0, 4), ("aux", AUX, 4, 3), ("out", OUT, 7, 1)):
    for n, g in enumerate(groups):
        RING[g] = (ring, n, first + n % count, n // count)
DOWN_BANK = [7, 4, 5, 6] + FFN_BANK
DRAINS = [(len(ACC) + 3 - b) // 4 for b in range(4)]
DRAINS += [sum(RING[g][2] == b for g in AUX) for b in (4, 5, 6)] + [len(OUT)]


def build(nc, x, rel_bias, norm_mix_g, w_in, conv_dw_w, conv_dw_b, conv_ln_g, conv_ln_b, q_norm_g,
          k_norm_g, ssm_conv_w, ssm_conv_b, dt_bias, a_log, d_skip, ssm_norm_g, w_out, norm_ffn_g,
          w_up, ffn_conv_w, ffn_conv_b, w_down, onehot, out):
    x, out = x[0], out[0]
    w_in, w_out, w_up, w_down = w_in[0], w_out[0], w_up[0], w_down[0]
    gdram = nc.dram_tensor("distance_table", (NH, NG), F32, kind="Internal").ap()

    with ExitStack() as ctx:
        base = (nc.sbuf_base + 63) // 64 * 64
        top = [base]

        def at(name, shape, dt, offset=None):
            size = (int(np.prod(shape[1:])) * (2 if dt == BF16 else 4) + 31) // 32 * 32
            if offset is None:
                offset = top[0]
                top[0] += size
            return nc.alloc_sbuf_tensor_at(name, shape, dt, offset=offset)

        def region(kb):
            o = top[0]
            top[0] += int(kb * 1024)
            return o

        K = 1024
        ident = at("ident", [P, P], F32)
        tri = at("tri", [P, P], F32)
        neg_l = at("neg_l", [P, P], F32)
        neg_q = at("neg_q", [P, P], F32)
        ones = at("ones", [P, P], F32)
        prm = at("prm", [P, N_PRM], F32)
        st = at("stats", [P, 816], F32)
        wraw = at("w_raw", [P, NSLOT, 2048], F32)
        whi = at("w_hi", [P, NSLOT, 2048], F32R)
        wlo = at("w_lo", [P, NSLOT, 2048], F32R)
        hhi = at("h_hi", [P, KD, SEQ], F32R)
        hlo = at("h_lo", [P, KD, SEQ], F32R)
        r2 = region(16)
        mix0 = top[0]
        r1, r3, r4, r5, r6, r7, rs = (region(kb) for kb in (16, 16, 16, 10.5, 16, 16, 8))
        x_sb = at("x_in", [P, NT, DM], F32, r2)
        xn = at("x_normed", [P, NT, DM], F32, r6)
        rows = at("param_rows", [P, 4, P], F32, rs)
        gm_row = at("gm_row", [P, DM], F32, r3)
        ws_raw = at("small_raw", [P, KD, ID + 12], F32, r4)
        ws_hi = at("small_hi", [P, KD, ID + 12], F32R, r4 + 4608)
        ws_lo = at("small_lo", [P, KD, ID + 12], F32R, r4 + 9216)
        oneh = at("onehot_sb", [NBUCKET, NG], F32, r7)
        relb = at("relb", [NBUCKET, NH], F32, r7 + 2560)
        gsb = at("gsb", [NH, NG], F32, r7 + 3 * K)
        jrev = at("jrev", [P, P], F32, r7 + 6 * K)
        trev = at("trev", [P, NH, 512], F32, r6)
        tbias = at("tbias", [P, NH, 512], F32, r2)
        iqT = at("iqT", [P, 2, SEQ], F32, r3)
        ikT = at("ikT", [P, SEQ], F32, r3 + 4 * K)
        iwT = at("iwdtT", [P, SEQ], F32, rs + 2 * K)
        relu = at("relu", [P, 2, 512], F32, r3 + 6 * K)
        rank = at("rank", [P, 3, 512], F32, r3 + 10 * K)
        selm = at("sel_mask", [P, 256 + 384 + 512], BF16, r5 + 8 * K)
        sqs = at("sq", [P, 2, 512], F32, rs + 4 * K)
        q_tok = at("q_tok", [P, NT, 512], F32, r1)
        k_tok = at("k_tok", [P, NT, 512], F32, r1 + 8 * K)
        qT = at("qT", [P, 4, SEQ], F32, r4)
        kT = at("kT", [P, 4, SEQ], F32, r4 + 8 * K)
        v_tok = at("v_tok", [P, NT, 512], F32, r5)
        tm = at("bias_masked", [P, 2, 512], F32, r1 + 8 * K)
        prob = at("prob", [P, 2, 512], F32, rs)
        probT = at("probT", [P, 2, 512], F32, rs + 4 * K)
        att_hi = at("att_hi", [P, 4, SEQ], F32R, r6)
        att_lo = at("att_lo", [P, 4, SEQ], F32R, r6 + 8 * K)
        dump = at("square_dump", [P, 512], F32)
        xbcT = at("xbcT", [P, 8, SEQ], F32, r3)
        z_tok = at("z_tok", [P, NT, 512], F32, r1)
        xs_tok = at("xs_tok", [P, NT, 512], F32, r1 + 8 * K)
        b_tok = at("b_tok", [P, 2, 256], F32, r5)
        state = at("state", [P, 512], F32, r5 + 2 * K)
        xd = at("xd", [P, 512], F32, r5 + 4 * K)
        xdd = at("xdd", [P, 512], F32, r5 + 6 * K)
        yb = at("yb", [P, 512], F32, r5 + 8 * K)
        xskip = at("xskip", [P, 512], F32)[:, :]
        tapped = [dump, xskip]
        gssm = at("gssm", [P, 512], F32)
        dec = at("dec", [P, SH, P], F32, rs)
        sct = at("sct", [P, SH, P], F32, rs + 4 * K)
        ssm_hi = at("ssm_hi", [P, 4, SEQ], F32R, r4)
        ssm_lo = at("ssm_lo", [P, 4, SEQ], F32R, r4 + 8 * K)
        u_in = at("u_in", [P, 4, SEQ], F32, r7)
        u_acc = at("u_acc", [P, 4, SEQ], F32, r7 + 8 * K)
        u_tok = at("u_tok", [P, NT, 512], F32, r7)
        conv_hi = at("conv_hi", [P, 4, SEQ], F32R, r7 + 8 * K)
        conv_lo = at("conv_lo", [P, NT, 4, P], F32R, r7)
        x2 = at("x2", [P, NT, DM], F32, r2)
        x2n = at("x2n", [P, NT, DM], F32, r3)
        gf_row = at("gf_row", [P, DM], F32, r5)
        ghi = at("g_hi", [P, NF, SEQ], F32R, mix0)
        glo = at("g_lo", [P, NF, SEQ], F32R, mix0 + NF * SEQ * 4)
        ffn = mix0 + 2 * NF * SEQ * 4
        fbuf = at("f", [P, 4, SEQ], F32, ffn)
        sg = at("sg", [P, 2, SEQ], F32, ffn + 8 * K)
        gg = at("gg", [P, 2, SEQ], F32, ffn + 12 * K)
        y_out = at("y_out", [P, 8, 512], F32, ffn)
        assert max(top[0], ffn + 16 * K) <= nc.sbuf_usable_end
        MIX = {"att": (att_hi, att_lo), "conv": (conv_hi, conv_lo), "ssm": (ssm_hi, ssm_lo)}

        free = [0]

        def col(n):
            free[0] += n
            return st[:, free[0] - n:free[0]]

        ssq, rstd = col(NT), col(NT)
        half_neg = col(32)
        iwdt = col(NT * 12).rearrange("p (t c) -> p t c", c=12)
        hbc = col(3 * SH).rearrange("p (w h) -> p w h", h=SH)
        aneg = col(SH)
        dtx, dte, dtu, dtl, dtv, dta = (col(32) for _ in range(6))
        m8 = col(24).rearrange("p (b e) -> p b e", e=8)
        ssqk, rqk = col(64), col(64)
        mn, psum_p, rp = col(NT * NH), col(NT * NH), col(NT * NH)
        csx, ecs = col(96), col(96)
        yss, yrs = col(NT), col(NT)
        bn6 = col(6)
        mv = col(2 * NT).rearrange("p (t c) -> p t c", c=2)
        lnr = col(NT)
        ssq2, rstd2 = col(2 * NT).rearrange("p (t h) -> p t h", h=2), col(NT)
        warm = col(2)
        assert free[0] <= 816

        bank = [ctx.enter_context(nc.psum_tensor(f"bank{b}", [P, 512], F32)) for b in range(8)]

        def sem(name):
            return ctx.enter_context(nc.semaphore(name))

        s_x = [sem(f"x_landed{t}") for t in range(NT)]
        s_const, s_rows, s_small, s_hbc, s_oneh = (
            sem(n) for n in ("consts_made", "rows_landed", "small_landed",
                             "head_params_landed", "onehot_landed"))
        s_gout, s_trev, s_x2, s_yout, s_gm, s_gf = (
            sem(n) for n in ("gtable_stored", "trev_landed", "x2_landed", "y_stored",
                             "gm_row_landed", "gf_row_landed"))
        w_landed = [sem(f"w_landed{n}") for n in range(NSLOT)]
        w_hi_ready, w_lo_ready = sem("w_hi_ready"), sem("w_lo_ready")
        pool_lo_ready = sem("pool_lo_ready")
        ws_hi_ready, ws_lo_ready = sem("ws_hi_ready"), sem("ws_lo_ready")
        acc_step, aux_done, out_done = sem("acc_step"), sem("aux_done"), sem("out_done")
        drained = [sem(f"drained{b}") for b in range(8)]
        dve_step, act_step, pool_step = sem("dve_step"), sem("act_step"), sem("pool_step")
        hi_evac = sem("hi_evac")
        ssq_ready, ms_ready, rstd_ready = sem("ssq_ready"), sem("ms_ready"), sem("rstd_ready")
        xn_ready = sem("xn_ready")
        sig_ready, glu_ready = sem("sig_ready"), sem("glu_ready")
        top_step = {b: sem(f"top_step{b}") for b in (1, 2, 3)}
        dw_taps = [sem(f"dw_taps{j}") for j in range(4)]
        dwp_ready = sem("dw_product_ready")
        relu_ready, relu_used, sel_ready = sem("relu_ready"), sem("relu_used"), sem("sel_ready")
        sq_used, qkms_ready, rqk_ready, qkn_ready = (
            sem(n) for n in ("sq_used", "qkms_ready", "rqk_ready", "qkn_ready"))
        tm_ready, exp_ready, rp_ready, prob_ready = (
            sem(n) for n in ("tm_ready", "exp_ready", "rp_ready", "prob_ready"))
        nx_ready, dte_ready, dtu_ready, dtl_ready, dta_ready = (
            sem(n) for n in ("nx_ready", "dte_ready", "dtu_ready", "dtl_ready", "dta_ready"))
        xbase_ready, xtap_ready, xbc_ready = sem("xbase_ready"), sem("xtap_ready"), sem("xbc_ready")
        z_ready = sem("z_ready")
        csx_ready, ecs_ready = sem("csx_ready"), sem("ecs_ready")
        seg_ready, dec_ready, sct_ready = sem("seg_ready"), sem("dec_ready"), sem("sct_ready")
        xd_ready = sem("xd_ready")
        yg_ready, yss_ready, yms_ready, yrs_ready, yn_ready = (
            sem(n) for n in ("yg_ready", "yss_ready", "yms_ready", "yrs_ready", "yn_ready"))
        state_ready = sem("state_ready")
        lnv_ready, lnr_ready = sem("lnv_ready"), sem("lnr_ready")
        us_ready, chi_ready, clo_ready = sem("us_ready"), sem("chi_ready"), sem("clo_ready")
        ssq2_ready, ms2a_ready, ms2_ready, rstd2_ready, x2n_ready = (
            sem(n) for n in ("ssq2_ready", "ms2a_ready", "ms2_ready", "rstd2_ready", "x2n_ready"))
        f_ready, ftap_ready, sg_ready, gg_ready, ghi_ready, glo_ready = (
            sem(n) for n in ("f_ready", "ftap_ready", "sg_ready", "gg_ready", "ghi_ready",
                             "glo_ready"))
        y_ready = sem("y_ready")

        block = ctx.enter_context(nc.Block())

        def ps(*key):
            return bank[RING[key][2]]

        def finished(eng, *key):
            ring, n = RING[key][:2]
            if ring in ("acc", "out"):
                eng.wait_ge(acc_step if ring == "acc" else out_done, STEP[key])
            else:
                eng.wait_ge(aux_done, n + 1)

        def evacuated(eng, *key):
            eng.wait_ge(drained[RING[key][2]], RING[key][3] + 1)

        def drain(ins, *key):
            ins.then_inc(drained[RING[key][2]], 1)

        def claim(eng, *key):
            if RING[key][3]:
                eng.wait_ge(drained[RING[key][2]], RING[key][3])

        def tap(eng, j, i):
            c = R_CW + 4 * (CONV_K - 1 - i) + j
            w = prm[:, c:c + 1]
            if i == 0:
                eng.wait_ge(glu_ready, j + 1)
                eng.tensor_scalar(u_acc[:, j, :], u_in[:, j, :], w,
                                  prm[:, R_CB + j:R_CB + j + 1], ALU.mult, ALU.add)\
                    .then_inc(dw_taps[j], 1)
            else:
                eng.wait_ge(dw_taps[j], i)
                eng.scalar_tensor_tensor(
                    out=u_acc[:, j, i:], in0=u_in[:, j, 0:SEQ - i], scalar=w,
                    in1=u_acc[:, j, i:], op0=ALU.mult, op1=ALU.add).then_inc(dw_taps[j], 1)

        def part_lo(eng, c, ready):
            cols = slice(0, POOL_COLS) if ready is pool_lo_ready else \
                slice(POOL_COLS if c in POOL_LO else 0, 2048)
            eng.wait_ge(w_hi_ready, c + 1)
            slot = c % NSLOT
            eng.tensor_tensor(wlo[:, slot, cols], wraw[:, slot, cols],
                              whi[:, slot, cols].bitcast(F32), ALU.subtract).then_inc(ready, 1)

        @block.sync
        def _(sp):
            def load(c):
                what, i = CHUNKS[c]
                if c >= NSLOT:
                    sp.wait_ge(w_lo_ready, c - NSLOT + 1)
                    if c - NSLOT in POOL_LO:
                        sp.wait_ge(pool_lo_ready, POOL_LO.index(c - NSLOT) + 1)
                slot = wraw[:, c % NSLOT, :]
                done = w_landed[c % NSLOT]
                if what in ("iq", "xbc"):
                    c0 = C_IQ if what == "iq" else C_XBC + 256 * i
                    src = w_in[:, c0:c0 + 256].rearrange("(k p) n -> p k n", p=P)
                    dst = slot.rearrange("p (k n) -> p k n", k=KD)
                    for a in (0, 4):
                        sp.dma_start(dst[:, a:a + 4], src[:, a:a + 4]).then_inc(done, 16)
                elif what in ("conv", "up"):
                    w, ca, cg = (w_in, C_CA, C_CG) if what == "conv" else (w_up, 0, D_FF)
                    dst = slot.rearrange("p (k s n) -> p k s n", k=KD, s=2)
                    for s, c0 in enumerate((cg, ca)):
                        src = w[:, c0 + P * i:c0 + P * i + P].rearrange("(k p) n -> p k n", p=P)
                        sp.dma_start(dst[:, :, s], src).then_inc(done, 16)
                elif what == "down":
                    dst = slot.rearrange("p (k n) -> p k n", k=2)
                    for k in range(2):
                        r = P * (2 * i + k)
                        sp.dma_start(dst[:, k], w_down[r:r + P, :]).then_inc(done, 16)
                else:
                    if what == "out":
                        src = w_out[P * MIX_TILE[i[0]]:P * (MIX_TILE[i[0]] + 4),
                                    512 * i[1]:512 * i[1] + 512]
                    else:
                        c0 = {"q": C_Q, "k": C_K, "v": C_V, "z": C_Z}[what]
                        src = w_in[512 * i:512 * i + 512, c0:c0 + 512]
                    src = src.rearrange("(k p) n -> p k n", p=P)
                    dst = slot.rearrange("p (k n) -> p k n", k=4)
                    for a in (0, 2):
                        sp.dma_start(dst[:, a:a + 2], src[:, a:a + 2]).then_inc(done, 16)

            def put_rows(r, v):
                sp.dma_start(rows[r % P:r % P + v.shape[0], r // P, :], v).then_inc(s_rows, 16)

            def vec(v):
                return v.rearrange("o (r c) -> (o r) c", c=P)

            for t in range(NT):
                sp.dma_start(x_sb[:, t, :], x[P * t:P * t + P, :]).then_inc(s_x[t], 16)

            load(0)
            wsrc = w_in.rearrange("(k p) n -> p k n", p=P)
            for c0, n, at_ in ((C_IK, ID, 0), (C_IW, NIH, ID), (C_DT, SH, ID + NIH)):
                sp.dma_start(ws_raw[:, :, at_:at_ + n], wsrc[:, :, c0:c0 + n]).then_inc(s_small, 16)
            sp.dma_start(oneh[:, :], onehot).then_inc(s_oneh, 16)
            sp.dma_start(relb[:, :], rel_bias).then_inc(s_oneh, 16)
            load(1)
            for w, v in enumerate((dt_bias, a_log, d_skip)):
                sp.dma_start(hbc[:, w, :], v.to_broadcast([P, SH])).then_inc(s_hbc, 16)
            sp.dma_start(gssm[:, :], ssm_norm_g.to_broadcast([P, 512])).then_inc(s_hbc, 16)
            put_rows(R_CB, vec(conv_dw_b))
            put_rows(R_LG, vec(conv_ln_g))
            put_rows(R_LB, vec(conv_ln_b))
            put_rows(R_SW, ssm_conv_w[0].rearrange("k (r c) -> (k r) c", c=P))
            put_rows(R_SB, vec(ssm_conv_b))
            put_rows(R_FB, vec(ffn_conv_b))
            for r, v in ((R_QG, q_norm_g), (R_KG, k_norm_g)):
                for u in range(2):
                    sp.dma_start(rows[r:r + 1, 0, HD * u:HD * u + HD], v)\
                        .then_inc(s_rows, 16)
            put_rows(P, conv_dw_w[0].rearrange("k (r c) -> (k r) c", c=P))
            fw = ffn_conv_w[0].rearrange("k (r c) -> (k r) c", c=P)
            put_rows(2 * P, fw[0:P])
            put_rows(3 * P, fw[P:FK * 2 * NF])
            for s in PLAN:
                if s[0] == "lo" and s[1] + NSLOT < UP0 + 2:
                    load(s[1] + NSLOT)
                elif s[0] == "gtab":
                    evacuated(sp, "gt", 0)
                    evacuated(sp, "gt", 1)
                    sp.dma_start(gdram, gsb[:, :]).then_inc(s_gout, 16)
                    sp.wait_ge(s_gout, 16)
                    finished(sp, "hT", NT - 1, 1)
                    src = bass.AP(gdram.tensor, 0, [[1, P], [NG, NH], [1, 512]])
                    sp.dma_start(trev[:, :, :], src).then_inc(s_trev, 16)
                elif s == ("xt", 0):
                    sp.wait_ge(tm_ready, NT * NH)
                    for t in range(NT):
                        sp.dma_start(x2[:, t, :], x[P * t:P * t + P, :]).then_inc(s_x2, 16)
                elif s == ("ssdT", NT - 1):
                    evacuated(sp, "yT", NT - 1)
                    sp.dma_start(gf_row[:, :], norm_ffn_g.to_broadcast([P, DM])).then_inc(s_gf, 16)

            with sp.Fori(0, NF // 2 - 1) as n:
                for s in range(2):
                    c = UP0 + 2 + s
                    sp.wait_ge(w_lo_ready, n * 2 + (c - NSLOT + 1))
                    dst = wraw[:, c % NSLOT, :].rearrange("p (k s n) -> p k s n", k=KD, s=2)
                    for v, c0 in enumerate((D_FF, 0)):
                        src = w_up[:, bass.ds(n * (2 * P) + (c0 + P * (2 + s)), P)]
                        sp.dma_start(dst[:, :, v], src.rearrange("(k p) n -> p k n", p=P))\
                            .then_inc(w_landed[c % NSLOT], 16)
            for c in range(DN0, len(CHUNKS)):
                load(c)
            for t in range(NT):
                for half in range(2):
                    sp.wait_ge(y_ready, 2 * t + half + 1)
                    sp.dma_start(out[P * t:P * t + P, 512 * half:512 * half + 512],
                                 y_out[:, 2 * t + half, :]).then_inc(s_yout, 16)
            sp.wait_ge(s_yout, 16 * 2 * NT)

        @block.gpsimd
        def _(pool):
            n_link = [0]

            def link(ins):
                n_link[0] += 1
                ins.then_inc(pool_step, 1)
                pool.wait_ge(pool_step, n_link[0])

            link(pool.memset(ident[:, :], 0.0))
            link(pool.affine_select(out=ident[:, :], in_=ident[:, :], compare_op=ALU.not_equal,
                                    fill=1.0, base=0, pattern=[[-1, P]], channel_multiplier=1))
            link(pool.memset(half_neg, -0.5))
            link(pool.memset(ones[:, :], 1.0))
            link(pool.affine_select(out=tri[:, :], in_=ones[:, :], compare_op=ALU.is_ge, fill=0.0,
                                    base=0, pattern=[[1, P]], channel_multiplier=-1))
            link(pool.memset(neg_l[:, :], 0.0))
            link(pool.memset(jrev[:, :], 0.0))
            link(pool.affine_select(out=neg_q[:, :], in_=neg_l[:, :], compare_op=ALU.is_ge,
                                    fill=MASKED, base=0, pattern=[[-1, P]], channel_multiplier=1))
            link(pool.affine_select(out=neg_l[:, :], in_=neg_l[:, :], compare_op=ALU.is_ge,
                                    fill=MASKED, base=0, pattern=[[1, P]], channel_multiplier=-1))
            pool.affine_select(out=jrev[:, :], in_=jrev[:, :], compare_op=ALU.not_equal, fill=1.0,
                               base=-(P - 1), pattern=[[1, P]], channel_multiplier=1)\
                .then_inc(s_const, 1)

            def inverse_root(out_, in_, ready):
                n = out_.free_size()
                pool.tensor_tensor(out_, in_, half_neg[:, 0:n], ALU.pow).then_inc(ready, 1)

            for s in PLAN:
                k = s[0]
                if k == "norm":
                    t = s[1]
                    pool.wait_ge(ms_ready, t + 1)
                    inverse_root(rstd[:, t:t + 1], ssq[:, t:t + 1], rstd_ready)
                elif k == "qkms":
                    which = "qk".index(s[1])
                    pool.wait_ge(qkms_ready, which + 1)
                    inverse_root(rqk[:, 32 * which:32 * which + 32],
                                 ssqk[:, 32 * which:32 * which + 32], rqk_ready)
                elif k == "score":
                    _, i, b, h = s
                    W = P * (b + 1)
                    if i == 0:
                        finished(pool, "qkT", "k", 3)
                        for hh in range(NH):
                            evacuated(pool, "tbias", hh)
                    if i >= 2:
                        evacuated(pool, "score", i - 2, *divmod(i - 2, NH))
                    if b:
                        pool.wait_ge(sel_ready, 3)
                    m = neg_q[:, :] if b == 0 else selm[:, SEL0[b]:SEL0[b] + W]
                    pool.tensor_tensor(tm[:, i % 2, 0:W], tbias[:, h, 384 - P * b:384 - P * b + W],
                                       m, ALU.add).then_inc(tm_ready, 1)
                elif k == "dw" and s[1] == DW_POOL:
                    _, j, i = s
                    if i == 0:
                        tap(pool, j, i)
                    else:
                        pool.wait_ge(dw_taps[j], i)
                        pool.wait_ge(dwp_ready, i)
                        pool.tensor_tensor(u_acc[:, j, i:], tapped[i % 2][:, 0:SEQ - i],
                                           u_acc[:, j, i:], ALU.add).then_inc(dw_taps[j], 1)
                elif k == "lo" and s[1] in POOL_LO:
                    part_lo(pool, s[1], pool_lo_ready)
                elif k == "seg":
                    t = s[1]
                    if t == 0:
                        finished(pool, "pv", NT - 1)
                        pool.wait_ge(dta_ready, 1)
                        pool.wait_ge(s_hbc, 64)
                        for tt in range(NT):
                            evacuated(pool, "xs", tt)
                        pool.wait_ge(ecs_ready, 1)
                        pool.wait_ge(dw_taps[DW_POOL], CONV_K)
                    else:
                        finished(pool, "yd", t - 1)
                        finished(pool, "st", t - 1)
                        pool.wait_ge(yg_ready, t)
                    v3 = xs_tok[:, t, :].rearrange("p (h c) -> p h c", h=SH)
                    x3, xx3, sk3 = (b_.rearrange("p (h c) -> p h c", h=SH)
                                    for b_ in (xd[:, :], xdd[:, :], xskip))

                    def per_head(ap):
                        return ap.unsqueeze(2).to_broadcast([P, SH, SP_])

                    pool.tensor_tensor(x3, v3, per_head(dtv[:, SH * t:SH * t + SH]), ALU.mult)\
                        .then_inc(xd_ready, 1)
                    pool.tensor_tensor(sk3, v3, per_head(hbc[:, 2, :]), ALU.mult)\
                        .then_inc(xd_ready, 1)
                    pool.wait_ge(xd_ready, 3 * t + 1)
                    pool.tensor_tensor(xx3, x3, per_head(ecs[:, 64 + SH * t:64 + SH * t + SH]),
                                       ALU.mult).then_inc(xd_ready, 1)
                elif k == "yms":
                    pool.wait_ge(yms_ready, s[1] + 1)
                    inverse_root(yrs[:, s[1]:s[1] + 1], yss[:, s[1]:s[1] + 1], yrs_ready)
                elif s[0] == "sq2" and s[2] == 1:
                    t = s[1]
                    pool.wait_ge(ms2_ready, t + 1)
                    inverse_root(rstd2[:, t:t + 1], ssq2[:, t, 0:1], rstd2_ready)
                elif k == "lnn":
                    pool.wait_ge(lnv_ready, s[1] + 1)
                    inverse_root(lnr[:, s[1]:s[1] + 1], mv[:, s[1], 1:2], lnr_ready)
        @block.scalar
        def _(act):
            n_link = [0]

            def link(ins):
                n_link[0] += 1
                ins.then_inc(act_step, 1)
                act.wait_ge(act_step, n_link[0])

            def high(out_, in_):
                act.activation(out_, in_, ACT.Copy).then_inc(hi_evac, 1)

            def take(dst, *key):
                finished(act, *key)
                drain(act.activation(dst, ps(*key)[:, :], ACT.Copy), *key)

            def split_hi(c):
                act.wait_ge(w_landed[c % NSLOT], 32 * (c // NSLOT + 1))
                if c >= NSLOT:
                    act.wait_ge(acc_step, STEP[("chunk", c - NSLOT)])
                act.activation(whi[:, c % NSLOT, :], wraw[:, c % NSLOT, :], ACT.Copy)\
                    .then_inc(w_hi_ready, 1)

            act.dma_start(gm_row[:, :], norm_mix_g.to_broadcast([P, DM])).then_inc(s_gm, 16)
            act.wait_ge(s_const, 1)
            act.activation(warm[:, 0:1], half_neg[:, 0:1], ACT.Square)

            def norm_hi(dst, key, t):
                for g in range(2):
                    finished(act, key, t, g)
                    high(dst[:, 4 * g:4 * g + 4, P * t:P * t + P],
                         ps(key, t, g)[:, :].rearrange("p (k q) -> p k q", k=4))

            for s in PLAN:
                k = s[0]
                if k == "prm":
                    finished(act, "prm")
                    drain(act.activation(prm[:, :], ps("prm")[:, 0:N_PRM], ACT.Copy), "prm")
                elif k == "gtab":
                    for i in range(2):
                        finished(act, "gt", i)
                        n = 512 if i == 0 else NG - 512
                        drain(act.activation(gsb[:, 512 * i:512 * i + n], ps("gt", i)[0:NH, 0:n],
                                             ACT.Copy), "gt", i)
                elif k == "norm":
                    t = s[1]
                    act.wait_ge(s_x[t], 16)
                    act.activation(xn[:, t, :], x_sb[:, t, :], ACT.Square,
                                   accum_out=ssq[:, t:t + 1]).then_inc(ssq_ready, 1)
                    if t:
                        norm_hi(hhi, "hT", t - 1)
                elif k == "wsplit":
                    norm_hi(hhi, "hT", NT - 1)
                    act.wait_ge(s_small, 48)
                    act.activation(ws_hi[:, :, :], ws_raw[:, :, :], ACT.Copy).then_inc(ws_hi_ready, 1)
                elif k == "ev":
                    _, what, i = s
                    if what == "ik":
                        finished(act, "ik", 0)
                        for lo_ in (0, ID):
                            link(act.activation(ikT[lo_:lo_ + ID, :], ps("ik", 0)[0:ID, :],
                                                ACT.Copy))
                        drain(act.activation(iwT[ID:ID + 12, :], ps("ik", 0)[ID:ID + 12, :],
                                             ACT.Copy), "ik", 0)
                        continue
                    dst = {"iq": iqT, "v": v_tok, "z": z_tok, "cg": u_acc, "ca": u_in}.get(what)
                    take(dst[:, i, :], what, i)
                elif k == "glu":
                    j = s[1]
                    evacuated(act, "cg", j)
                    act.activation(u_acc[:, j, :], u_acc[:, j, :], ACT.Sigmoid).then_inc(sig_ready, 1)
                elif s == ("dt", 0):
                    act.wait_ge(nx_ready, 1)
                    act.activation(dte, dte, ACT.Exp).then_inc(dte_ready, 1)
                    act.wait_ge(s_hbc, 64)
                    act.activation(aneg, hbc[:, 1, :], ACT.Exp).then_inc(dte_ready, 1)
                elif s == ("dt", 1):
                    act.wait_ge(dtu_ready, 1)
                    act.activation(dtl, dtu, ACT.Ln).then_inc(dtl_ready, 1)
                elif k == "hi":
                    split_hi(s[1])
                elif k == "tbias":
                    finished(act, *s)
                    drain(act.activation(tbias[:, s[1], :], ps(*s)[:, :], ACT.Copy), *s)
                elif k == "idx":
                    _, b, h = s
                    i = (b - 1) * NIH + h
                    W = P * (b + 1)
                    finished(act, *s)
                    if i >= 2:
                        act.wait_ge(relu_used, i - 1)
                    act.activation(relu[:, i % 2, 0:W], ps(*s)[:, 0:W], ACT.Relu,
                                   scale=ID ** -0.5 * NIH ** -0.5)\
                        .then_inc(drained[RING[s][2]], 1)
                elif k == "qkev":
                    _, what, t = s
                    tok = q_tok if what == "q" else k_tok
                    i = NT * "qk".index(what) + t
                    finished(act, what, t)
                    link(act.activation(tok[:, t, :], ps(what, t)[:, :], ACT.Copy))
                    if i >= 2:
                        act.wait_ge(sq_used, i - 1)
                    act.activation(sqs[:, i % 2, :], ps(what, t)[:, :], ACT.Square)\
                        .then_inc(drained[RING[(what, t)][2]], 1)
                elif k == "qkT":
                    dst, g = (qT, R_QG) if s[1] == "q" else (kT, R_KG)
                    finished(act, *s)
                    evacuated(act, "prm")
                    drain(act.activation(dst[:, s[2], :], ps(*s)[:, :], ACT.Copy,
                                         scale=prm[:, g:g + 1]), *s)
                elif k == "xbase":
                    m = s[1]
                    finished(act, "xbc", m)
                    act.activation(xbcT[:, m, :], ps("xbc", m)[:, :], ACT.Identity,
                                   bias=prm[:, R_SB + m:R_SB + m + 1],
                                   scale=prm[:, R_SW + 24 + m:R_SW + 25 + m])\
                        .then_inc(xbase_ready, 1)
                elif k == "silux":
                    for m in range(8):
                        evacuated(act, "xbc", m)
                        act.activation(xbcT[:, m, :], xbcT[:, m, :], ACT.Silu).then_inc(xbc_ready, 1)
                elif k == "siluz":
                    for t in range(NT):
                        evacuated(act, "z", t)
                    act.activation(z_tok[:, :, :], z_tok[:, :, :], ACT.Silu).then_inc(z_ready, 1)
                elif k == "score":
                    _, i, b, h = s
                    evacuated(act, *s)
                    p = prob[:, i % 2, 0:P * (b + 1)]
                    act.activation(p, p, ACT.Exp, bias=mn[:, i:i + 1], scale=-1.0,
                                   accum_out=psum_p[:, i:i + 1]).then_inc(exp_ready, 1)
                elif k == "share":
                    i = s[1]
                    b = i // NH
                    act.wait_ge(rp_ready, i + 1)
                    p = prob[:, i % 2, 0:P * (b + 1)]
                    act.activation(p, p, ACT.Copy, scale=rp[:, i:i + 1]).then_inc(prob_ready, 1)
                elif k == "evT":
                    i = s[1]
                    b = i // NH
                    s = ("turn", i, b, i % NH)
                    finished(act, *s)
                    if i >= 2:
                        act.wait_ge(out_done, i - 1)
                    W = P * (b + 1)
                    drain(act.activation(probT[:, i % 2, 0:W], ps(*s)[:, 0:W], ACT.Copy), *s)
                elif k == "attout":
                    b = s[1]
                    finished(act, "pv", b)
                    high(att_hi[:, :, P * b:P * b + P],
                         ps("pv", b)[:, :].rearrange("p (j q) -> p j q", j=4))
                elif k == "xt":
                    finished(act, "xs", s[1])
                    drain(act.activation(xs_tok[:, s[1], :], ps("xs", s[1])[:, :], ACT.Copy),
                          "xs", s[1])
                elif k == "cs":
                    act.wait_ge(csx_ready, 1)
                    act.activation(ecs, csx, ACT.Exp).then_inc(ecs_ready, 1)
                elif k == "seg":
                    t = s[1]
                    for g in range(SG):
                        act.wait_ge(seg_ready, SG * t + g + 1)
                        d = dec[:, 4 * g:4 * g + 4, :]
                        act.activation(d, d, ACT.Exp).then_inc(dec_ready, 1)
                elif k == "ssd":
                    t = s[1]
                    if t < NT - 1:
                        finished(act, "bt", t)
                        drain(act.activation(b_tok[:, t % 2, :], ps("bt", t)[:, 0:256], ACT.Copy),
                              "bt", t)
                elif k == "ysq":
                    t = s[1]
                    act.wait_ge(yg_ready, t + 1)
                    if t == 0:
                        act.wait_ge(dw_taps[DW_POOL], CONV_K)
                    act.activation(dump[:, :], yb[:, :], ACT.Square,
                                   accum_out=yss[:, t:t + 1]).then_inc(yss_ready, 1)
                elif k == "ssdT":
                    t = s[1]
                    finished(act, "yT", t)
                    high(ssm_hi[:, :, P * t:P * t + P],
                         ps("yT", t)[:, :].rearrange("p (j q) -> p j q", j=4))
                elif k == "dwp":
                    _, j, i = s
                    c = R_CW + 4 * (CONV_K - 1 - i) + j
                    if i > 2:
                        act.wait_ge(dw_taps[j], i - 1)
                    elif i == 1:
                        act.wait_ge(glu_ready, j + 1)
                    act.activation(tapped[i % 2][:, 0:SEQ - i], u_in[:, j, 0:SEQ - i], ACT.Copy,
                                   scale=prm[:, c:c + 1]).then_inc(dwp_ready, 1)
                elif k == "sq2":
                    _, t, half = s
                    evacuated(act, "wo", "ssm", half, t)
                    act.activation(dump[:, :], x2[:, t, 512 * half:512 * half + 512], ACT.Square,
                                   accum_out=ssq2[:, t, half:half + 1]).then_inc(ssq2_ready, 1)
                elif k == "h2ev":
                    norm_hi(hhi, "h2T", s[1])
                elif k == "lnT":
                    j = s[1]
                    finished(act, *s)
                    v = u_tok[:, :, P * j:P * j + P]
                    drain(act.activation(v, ps(*s)[:, :].rearrange("p (t q) -> p t q", t=NT),
                                         ACT.Silu,
                                         bias=prm[:, R_LB + j:R_LB + j + 1],
                                         scale=prm[:, R_LG + j:R_LG + j + 1]), *s)
                    evacuated(act, *s)
                    act.activation(conv_hi[:, j, :].rearrange("p (t q) -> p t q", t=NT), v,
                                   ACT.Copy).then_inc(chi_ready, 1)

            act.wait_ge(s_const, 1)
            act.activation(warm[:, 1:2], half_neg[:, 0:1], ACT.Silu)

            with act.Fori(0, NF // 2) as n:
                for s in range(2):
                    c = UP0 + s + 1
                    act.wait_ge(w_landed[c % NSLOT], n * 32 + 32 * (c // NSLOT + 1))
                    if s == 0:
                        act.wait_ge(acc_step, n * 4 + STEP0)
                    else:
                        act.wait_ge(acc_step, n * 4 + STEP0 + 2)
                    act.activation(whi[:, c % NSLOT, :], wraw[:, c % NSLOT, :], ACT.Copy)\
                        .then_inc(w_hi_ready, 1)
                    act.wait_ge(gg_ready, n * 2 + (s + 1))
                    for v in range(2):
                        act.wait_ge(acc_step, n * 4 + STEP0 + 2 * s + v + 1)
                        tile = n * 2 + (s + (NF if v == 0 else 0))
                        act.activation(fbuf[:, 2 * s + v, :],
                                       bank[FFN_BANK[2 * s + v]][:, :], ACT.Identity,
                                       bias=prm[:, bass.ds(tile + R_FB, 1)],
                                       scale=prm[:, bass.ds(tile + (R_FW + 2 * 2 * NF), 1)])\
                            .then_inc(f_ready, 1)
                    act.wait_ge(drained[FFN_BANK[2 * s]], n + (ROUND0[2 * s] + 1))
                    act.activation(sg[:, s, :], fbuf[:, 2 * s, :], ACT.Silu).then_inc(sg_ready, 1)
                    act.wait_ge(gg_ready, n * 2 + (s + 2))
                    act.activation(ghi[:, bass.ds(n * 2 + s, 1), :],
                                   gg[:, s:s + 1, :], ACT.Copy).then_inc(ghi_ready, 1)
            for c in range(DN0 + 1, len(CHUNKS)):
                split_hi(c)

        @block.vector
        def _(dve):
            n_link = [0]

            def link(ins):
                n_link[0] += 1
                ins.then_inc(dve_step, 1)
                dve.wait_ge(dve_step, n_link[0])

            def wait_high(key):
                dve.wait_ge(hi_evac, HIGH.index(key) + 1)

            def norm_lo(key, t):
                for g in range(2):
                    dve.wait_ge(hi_evac, HIGH.index((key, t, g)) + 1)
                    c = (slice(None), slice(4 * g, 4 * g + 4), slice(P * t, P * t + P))
                    drain(dve.tensor_tensor(hlo[c], ps(key, t, g)[:, :]
                                            .rearrange("p (k q) -> p k q", k=4),
                                            hhi[c].bitcast(F32), ALU.subtract), key, t, g)

            for s in PLAN:
                k = s[0]
                if k == "norm":
                    t = s[1]
                    c = ssq[:, t:t + 1]
                    dve.wait_ge(ssq_ready, t + 1)
                    dve.tensor_scalar(c, c, 1.0 / DM, EPS, ALU.mult, ALU.add).then_inc(ms_ready, 1)
                    if t == 0:
                        dve.wait_ge(s_gm, 16)
                    dve.wait_ge(rstd_ready, t + 1)
                    dve.scalar_tensor_tensor(out=xn[:, t, :], in0=x_sb[:, t, :],
                                             scalar=rstd[:, t:t + 1], in1=gm_row[:, :],
                                             op0=ALU.mult, op1=ALU.mult).then_inc(xn_ready, 1)
                    if t:
                        norm_lo("hT", t - 1)
                elif k == "wsplit":
                    norm_lo("hT", NT - 1)
                    dve.wait_ge(ws_hi_ready, 1)
                    dve.tensor_tensor(ws_lo[:, :, :], ws_raw[:, :, :], ws_hi[:, :, :].bitcast(F32),
                                      ALU.subtract).then_inc(ws_lo_ready, 1)
                elif s == ("dt", 0):
                    finished(dve, "iwT")
                    drain(dve.tensor_copy(iwdt, ps("iwT")[:, 0:12 * NT]
                                          .rearrange("p (t c) -> p t c", c=12)), "iwT")
                    evacuated(dve, "iwT")
                    dve.wait_ge(s_hbc, 64)
                    x3 = dtx.rearrange("p (t h) -> p t h", h=SH)
                    link(dve.tensor_tensor(x3, iwdt[:, :, NIH:],
                                           hbc[:, 0:1, :].to_broadcast([P, NT, SH]), ALU.add))
                    link(dve.tensor_scalar(dte, dtx, -1.0, None, ALU.mult))
                    dve.tensor_tensor(dte, dtx, dte, ALU.min).then_inc(nx_ready, 1)
                elif s == ("dt", 1):
                    dve.wait_ge(dte_ready, 1)
                    dve.tensor_scalar(dtu, dte, 1.0, None, ALU.add).then_inc(dtu_ready, 1)
                elif s == ("dt", 2):
                    dve.wait_ge(dtu_ready, 1)
                    dve.wait_ge(dtl_ready, 1)
                    link(dve.tensor_scalar(dta, dtu, -1.0, None, ALU.add))
                    link(dve.tensor_scalar(dtv, dta, 1e-30, None, ALU.max))
                    link(dve.reciprocal(dtv, dtv))
                    link(dve.tensor_tensor(dtv, dtv, dte, ALU.mult))
                    link(dve.tensor_tensor(dtv, dtv, dtl, ALU.mult))
                    link(dve.scalar_tensor_tensor(out=dta, in0=dta, scalar=0.0, in1=dte,
                                                  op0=ALU.is_equal, op1=ALU.mult))
                    link(dve.tensor_tensor(dtv, dtv, dta, ALU.add))
                    link(dve.scalar_tensor_tensor(out=dtv, in0=dtx, scalar=0.0, in1=dtv,
                                                  op0=ALU.max, op1=ALU.add))
                    dve.wait_ge(dte_ready, 2)
                    dve.scalar_tensor_tensor(
                        out=dta.rearrange("p (t h) -> p t h", h=SH),
                        in0=dtv.rearrange("p (t h) -> p t h", h=SH), scalar=-1.0,
                        in1=aneg.unsqueeze(1).to_broadcast([P, NT, SH]), op0=ALU.mult,
                        op1=ALU.mult).then_inc(dta_ready, 1)
                elif k == "lo":
                    part_lo(dve, s[1], w_lo_ready)
                elif k == "glu":
                    j = s[1]
                    evacuated(dve, "ca", j)
                    dve.wait_ge(sig_ready, j + 1)
                    dve.tensor_tensor(u_in[:, j, :], u_in[:, j, :], u_acc[:, j, :], ALU.mult)\
                        .then_inc(glu_ready, 1)
                elif k == "dw" and s[1] != DW_POOL:
                    tap(dve, *s[1:])
                elif k == "idx":
                    _, b, h = s
                    i = (b - 1) * NIH + h
                    W = P * (b + 1)
                    evacuated(dve, *s)
                    r, iw = rank[:, b - 1, 0:W], iwdt[:, b, h:h + 1]
                    if h == 0:
                        dve.tensor_scalar(r, relu[:, i % 2, 0:W], iw, 0.0, ALU.mult, ALU.add)\
                            .then_inc(relu_used, 1)
                    else:
                        dve.wait_ge(relu_used, i)
                        dve.scalar_tensor_tensor(out=r, in0=relu[:, i % 2, 0:W], scalar=iw, in1=r,
                                                 op0=ALU.mult, op1=ALU.add).then_inc(relu_used, 1)
                    if h == NIH - 1:
                        dve.wait_ge(relu_used, i + 1)
                        d = rank[:, b - 1, W - P:W]
                        link(dve.tensor_tensor(d, d, neg_q[:, :], ALU.add))
                elif k == "topmax":
                    _, b, r = s
                    if r:
                        dve.wait_ge(top_step[b], 2 * r)
                    dve.max(m8[:, b - 1, :], rank[:, b - 1, 0:P * (b + 1)]).then_inc(top_step[b], 1)
                elif k == "topmark":
                    _, b, r = s
                    c = rank[:, b - 1, 0:P * (b + 1)]
                    dve.wait_ge(top_step[b], 2 * r + 1)
                    dve.match_replace(c, m8[:, b - 1, :], c, TAKEN).then_inc(top_step[b], 1)
                elif k == "sel":
                    for b in (1, 2, 3):
                        W = P * (b + 1)
                        dve.wait_ge(top_step[b], 2 * (TOPK // 8))
                        dve.tensor_scalar(selm[:, SEL0[b]:SEL0[b] + W], rank[:, b - 1, 0:W],
                                          0.5 * (MASKED + TAKEN), MASKED, ALU.is_gt, ALU.mult)\
                            .then_inc(sel_ready, 1)
                elif k == "qkev":
                    _, what, t = s
                    i = NT * "qk".index(what) + t
                    evacuated(dve, what, t)
                    dve.tensor_reduce(ssqk[:, NH * i:NH * i + NH],
                                      sqs[:, i % 2, :].rearrange("p (h c) -> p h c", h=NH),
                                      AX_X, ALU.add).then_inc(sq_used, 1)
                elif k == "qkms":
                    w = "qk".index(s[1])
                    dve.wait_ge(sq_used, NT * (w + 1))
                    a, b = (1.0, HD * EPS) if s[1] == "q" else (1.0 / HD, EPS)
                    c = ssqk[:, 32 * w:32 * w + 32]
                    dve.tensor_scalar(c, c, a, b, ALU.mult, ALU.add).then_inc(qkms_ready, 1)
                elif k == "qkn":
                    w = "qk".index(s[1])
                    tok = q_tok if s[1] == "q" else k_tok
                    dve.wait_ge(rqk_ready, w + 1)
                    for t in range(NT):
                        v3 = tok[:, t, :].rearrange("p (h c) -> p h c", h=NH)
                        c = 32 * w + NH * t
                        dve.tensor_tensor(v3, v3, rqk[:, c:c + NH].unsqueeze(2)
                                          .to_broadcast([P, NH, HD]), ALU.mult).then_inc(qkn_ready, 1)
                elif k == "score":
                    _, i, b, h = s
                    W = P * (b + 1)
                    finished(dve, *s)
                    dve.wait_ge(tm_ready, i + 1)
                    if i >= 2:
                        finished(dve, "turn", i - 2, *divmod(i - 2, NH))
                    dve.tensor_tensor_reduce(prob[:, i % 2, 0:W], ps(*s)[:, 0:W], tm[:, i % 2, 0:W],
                                             -1.0, 3.4e38, ALU.add, ALU.min, mn[:, i:i + 1])\
                        .then_inc(drained[RING[s][2]], 1)
                elif k == "share":
                    i = s[1]
                    dve.wait_ge(exp_ready, i + 1)
                    dve.reciprocal(rp[:, i:i + 1], psum_p[:, i:i + 1]).then_inc(rp_ready, 1)
                elif k == "attout":
                    b = s[1]
                    wait_high(s)
                    q = slice(P * b, P * b + P)
                    drain(dve.tensor_tensor(att_lo[:, :, q],
                                            ps("pv", b)[:, :].rearrange("p (j q) -> p j q", j=4),
                                            att_hi[:, :, q].bitcast(F32), ALU.subtract), "pv", b)
                elif k == "xtap":
                    _, m, i = s
                    c = R_SW + 8 * (SK - 1 - i) + m
                    dve.wait_ge(xbase_ready, m + 1)
                    if i > 1:
                        dve.wait_ge(xtap_ready, 2 * m + i - 1)
                    ins = dve.scalar_tensor_tensor(
                        out=xbcT[:, m, i:], in0=ps("xbc", m)[:, 0:SEQ - i], scalar=prm[:, c:c + 1],
                        in1=xbcT[:, m, i:], op0=ALU.mult, op1=ALU.add)
                    if i < SK - 1:
                        ins.then_inc(xtap_ready, 1)
                    else:
                        drain(ins, "xbc", m)
                elif k == "cs":
                    finished(dve, "cs")
                    drain(dve.tensor_copy(csx[:, 0:64], ps("cs")[:, 0:64]), "cs")
                    evacuated(dve, "cs")
                    dve.tensor_tensor(csx[:, 64:96], csx[:, 32:64], csx[:, 0:32], ALU.subtract)\
                        .then_inc(csx_ready, 1)
                elif k == "seg":
                    t = s[1]
                    for g in range(SG):
                        d = dec[:, 4 * g:4 * g + 4, :]
                        finished(dve, "csr", t, g)
                        dve.wait_ge(csx_ready, 1)
                        if t:
                            evacuated(dve, "gt2", t - 1)
                        c = SH * t + 4 * g
                        drain(dve.tensor_tensor(
                            d, ps("csr", t, g)[:, :].rearrange("p (h l) -> p h l", h=4),
                            csx[:, c:c + 4].unsqueeze(2).to_broadcast([P, 4, P]), ALU.subtract),
                            "csr", t, g)
                        evacuated(dve, "csr", t, g)
                        dve.tensor_tensor(d, d, neg_l[:, :].unsqueeze(1).to_broadcast([P, 4, P]),
                                          ALU.add).then_inc(seg_ready, 1)
                elif k == "sct":
                    t = s[1]
                    if t:
                        finished(dve, "yd", t - 1)
                    finished(dve, "gt2", t)
                    for g in range(SG):
                        dve.wait_ge(dec_ready, SG * t + g + 1)
                        ins = dve.tensor_tensor(
                            sct[:, 4 * g:4 * g + 4, :],
                            ps("gt2", t)[:, P * g:P * g + P].unsqueeze(1).to_broadcast([P, 4, P]),
                            dec[:, 4 * g:4 * g + 4, :], ALU.mult)
                        if g == SG - 1:
                            drain(ins, "gt2", t)
                elif k == "ssdout":
                    t = s[1]
                    y3 = yb[:, :].rearrange("p (h c) -> p h c", h=SH)
                    if t:
                        finished(dve, "yT", t - 1)
                        finished(dve, "yo", t)
                        drain(dve.tensor_tensor(
                            y3, ps("yo", t)[:, :].rearrange("p (h c) -> p h c", h=SH),
                            ecs[:, SH * t:SH * t + SH].unsqueeze(2).to_broadcast([P, SH, SP_]),
                            ALU.mult), "yo", t)
                        evacuated(dve, "yo", t)
                    finished(dve, "yd", t)
                    dve.wait_ge(xd_ready, 3 * t + 2)
                    other = yb[:, :] if t else xskip
                    drain(dve.tensor_tensor(yb[:, :], ps("yd", t)[:, :], other, ALU.add),
                          "yd", t)
                    evacuated(dve, "yd", t)
                    if t:
                        link(dve.tensor_tensor(yb[:, :], yb[:, :], xskip, ALU.add))
                    dve.wait_ge(z_ready, 1)
                    dve.tensor_tensor(yb[:, :], yb[:, :], z_tok[:, t, :], ALU.mult)\
                        .then_inc(yg_ready, 1)
                    if t < NT - 1:
                        s3 = state[:, :].rearrange("p (h c) -> p h c", h=SH)
                        if t:
                            c = 32 + SH * t
                            link(dve.tensor_tensor(s3, s3, ecs[:, c:c + SH].unsqueeze(2)
                                                   .to_broadcast([P, SH, SP_]), ALU.mult))
                        finished(dve, "st", t)
                        if t:
                            drain(dve.tensor_tensor(state[:, :], ps("st", t)[:, :], state[:, :],
                                                    ALU.add), "st", t)
                        else:
                            drain(dve.tensor_copy(state[:, :], ps("st", t)[:, :]), "st", t)
                elif k == "yms":
                    t = s[1]
                    dve.wait_ge(yss_ready, t + 1)
                    dve.tensor_scalar(yss[:, t:t + 1], yss[:, t:t + 1], 1.0 / 512, EPS, ALU.mult,
                                      ALU.add).then_inc(yms_ready, 1)
                elif k == "yn":
                    t = s[1]
                    dve.wait_ge(yrs_ready, t + 1)
                    dve.scalar_tensor_tensor(out=yb[:, :], in0=yb[:, :], scalar=yrs[:, t:t + 1],
                                             in1=gssm[:, :], op0=ALU.mult, op1=ALU.mult)\
                        .then_inc(yn_ready, 1)
                elif k == "ssdT":
                    t = s[1]
                    wait_high(s)
                    q = slice(P * t, P * t + P)
                    drain(dve.tensor_tensor(ssm_lo[:, :, q],
                                            ps("yT", t)[:, :].rearrange("p (j q) -> p j q", j=4),
                                            ssm_hi[:, :, q].bitcast(F32), ALU.subtract), "yT", t)
                elif k == "ln":
                    t = s[1]
                    finished(dve, *s)
                    link(dve.bn_stats(bn6, ps(*s)[:, :]))
                    link(dve.bn_aggr(mv[:, t, :], bn6))
                    dve.tensor_scalar(mv[:, t, 1:2], mv[:, t, 1:2], EPS, None, ALU.add)\
                        .then_inc(lnv_ready, 1)
                elif k == "sq2":
                    _, t, half = s
                    c = ssq2[:, t, 0:1]
                    dve.wait_ge(ssq2_ready, SQ2.index(s) + 1)
                    if half == 0:
                        dve.tensor_scalar(c, c, 1.0 / DM, EPS, ALU.mult, ALU.add)\
                            .then_inc(ms2a_ready, 1)
                    else:
                        dve.wait_ge(ms2a_ready, t + 1)
                        dve.tensor_scalar(c, ssq2[:, t, 1:2], 1.0 / DM, c, ALU.mult, ALU.add)\
                            .then_inc(ms2_ready, 1)
                elif k == "norm2":
                    t = s[1]
                    dve.wait_ge(rstd2_ready, t + 1)
                    dve.wait_ge(s_gf, 16)
                    for half in range(2):
                        c = slice(512 * half, 512 * half + 512)
                        evacuated(dve, "wo", "ssm", half, t)
                        dve.scalar_tensor_tensor(out=x2n[:, t, c], in0=x2[:, t, c],
                                                 scalar=rstd2[:, t:t + 1], in1=gf_row[:, c],
                                                 op0=ALU.mult, op1=ALU.mult).then_inc(x2n_ready, 1)
                elif k == "h2ev":
                    norm_lo("h2T", s[1])
                elif k == "lnn":
                    t = s[1]
                    dve.wait_ge(lnr_ready, t + 1)
                    for j in range(4):
                        dve.wait_ge(dw_taps[j], CONV_K)
                    drain(dve.tensor_scalar(u_tok[:, t, :], ps("ln", t)[:, :], mv[:, t, 0:1],
                                            lnr[:, t:t + 1], ALU.subtract, ALU.mult), "ln", t)
                elif k == "lnT":
                    j = s[1]
                    dve.wait_ge(chi_ready, j + 1)
                    dve.tensor_tensor(conv_lo[:, :, j, :], u_tok[:, :, P * j:P * j + P],
                                      conv_hi[:, j, :].bitcast(F32)
                                      .rearrange("p (t q) -> p t q", t=NT), ALU.subtract)\
                        .then_inc(clo_ready, 1)
                elif k == "wo":
                    _, g, half, t = s
                    order = list(MIX_TILE)
                    finished(dve, *s)
                    if g == "att":
                        dve.wait_ge(s_x2, 16 * NT)
                    else:
                        evacuated(dve, "wo", order[order.index(g) - 1], half, t)
                    xx = x2[:, t, 512 * half:512 * half + 512]
                    drain(dve.tensor_tensor(xx, ps(*s)[:, :], xx, ALU.add), *s)

            dve.sem_inc(gg_ready, 1)
            dve.sem_inc(glo_ready, 1)
            with dve.Fori(0, NF // 2) as n:
                for s in range(2):
                    c = UP0 + s + 1
                    dve.wait_ge(w_hi_ready, n * 2 + (c + 1))
                    dve.tensor_tensor(wlo[:, c % NSLOT, :], wraw[:, c % NSLOT, :],
                                      whi[:, c % NSLOT, :].bitcast(F32), ALU.subtract)\
                        .then_inc(w_lo_ready, 1)
                    for v in range(2):
                        dve.wait_ge(f_ready, n * 4 + (2 * s + v + 1))
                        tile = n * 2 + (s + (NF if v == 0 else 0))
                        for i in range(1, FK):
                            ins = dve.scalar_tensor_tensor(
                                out=fbuf[:, 2 * s + v, i:],
                                in0=bank[FFN_BANK[2 * s + v]][:, 0:SEQ - i],
                                scalar=prm[:, bass.ds(tile + (R_FW + 2 * NF * (FK - 1 - i)), 1)],
                                in1=fbuf[:, 2 * s + v, i:], op0=ALU.mult, op1=ALU.add)
                            if i == 1:
                                ins.then_inc(ftap_ready, 1)
                                dve.wait_ge(ftap_ready, n * 4 + (2 * s + v + 1))
                            else:
                                ins.then_inc(drained[FFN_BANK[2 * s + v]], 1)
                    dve.wait_ge(sg_ready, n * 2 + (s + 1))
                    dve.wait_ge(drained[FFN_BANK[2 * s + 1]], n + (ROUND0[2 * s + 1] + 1))
                    dve.wait_ge(glo_ready, n * 2 + (s + 1))
                    dve.tensor_tensor(gg[:, s, :], fbuf[:, 2 * s + 1, :], sg[:, s, :], ALU.mult)\
                        .then_inc(gg_ready, 1)
                    dve.wait_ge(ghi_ready, n * 2 + (s + 1))
                    jj = n * 2 + s
                    dve.tensor_tensor(glo[:, bass.ds(jj, 1), :], gg[:, s:s + 1, :],
                                      ghi[:, bass.ds(jj, 1), :].bitcast(F32), ALU.subtract)\
                        .then_inc(glo_ready, 1)
            for c in range(DN0 + 1, len(CHUNKS)):
                part_lo(dve, c, w_lo_ready)
            for t in range(NT):
                for half in range(2):
                    i = 2 * t + half
                    dve.wait_ge(acc_step, STEP[("chunk", len(CHUNKS) - 2)] + i + 1)
                    dve.tensor_tensor(y_out[:, i, :], bank[DOWN_BANK[i]][:, :],
                                      x2[:, t, 512 * half:512 * half + 512], ALU.add)\
                        .then_inc(y_ready, 1)

        @block.tensor
        def _(pe):
            def product(o, terms, first=True, last=True):
                n = len(terms)
                for i, (whi_, wlo_, mhi, mlo) in enumerate(terms):
                    for q, (a, b) in enumerate(((whi_, mhi), (whi_, mlo), (wlo_, mhi))):
                        ins = pe.matmul(o, a, b, start=first and i == 0 and q == 0,
                                        stop=last and i == n - 1 and q == 2)
                return ins

            def turn(o, in_):
                n = in_.shape[0]
                return pe.transpose(o, in_, ident[0:n, 0:n])

            def channels(c, v, o, ks):
                h, l = (w[:, c % NSLOT, :].rearrange("p (k s n) -> p k s n", k=KD, s=2)
                        for w in (whi, wlo))
                return product(o, [(h[:, kk, v], l[:, kk, v], hhi[:, kk, :], hlo[:, kk, :])
                                   for kk in ks], first=ks[0] == 0, last=ks[-1] == KD - 1)

            def turn_norm(src, key, t):
                for g in range(2):
                    if key == "h2T":
                        pe.wait_ge(x2n_ready, 2 * t + g + 1)
                    claim(pe, key, t, g)
                    for kk in range(4):
                        ins = turn(ps(key, t, g)[:, P * kk:P * kk + P],
                                   src[:, t, P * (4 * g + kk):P * (4 * g + kk) + P])
                    ins.then_inc(aux_done, 1)

            for s in PLAN:
                k = s[0]
                if k == "norm":
                    if s[1] == 0:
                        pe.wait_ge(s_const, 1)
                    pe.wait_ge(xn_ready, s[1] + 1)
                    turn_norm(xn, "hT", s[1])
                elif k == "h2":
                    turn_norm(x2n, "h2T", s[1])
                elif k == "prm":
                    pe.wait_ge(s_const, 1)
                    pe.wait_ge(s_rows, 16 * 13)
                    claim(pe, "prm")
                    c = 0
                    for i, n in enumerate((N_ROW0, 4 * CONV_K, P, FK * 2 * NF - P)):
                        ins = turn(ps(*s)[:, c:c + n], rows[0:n, i, :])
                        c += n
                    ins.then_inc(aux_done, 1)
                elif k == "small":
                    pe.wait_ge(ws_lo_ready, 1)
                    claim(pe, "ik", 0)
                    product(ps("ik", 0)[0:ID + 12, :],
                            [(ws_hi[:, kk, :], ws_lo[:, kk, :], hhi[:, kk, :], hlo[:, kk, :])
                             for kk in range(KD)]).then_inc(aux_done, 1)
                elif k == "iwT":
                    evacuated(pe, "ik", 0)
                    claim(pe, *s)
                    for t in range(NT):
                        ins = pe.transpose(ps(*s)[:, 12 * t:12 * t + 12],
                                           iwT[ID:ID + 12, P * t:P * t + P],
                                           ident[ID:ID + 12, ID:ID + 12])
                    ins.then_inc(aux_done, 1)
                elif k == "gtab":
                    pe.wait_ge(s_oneh, 32)
                    for i in range(2):
                        claim(pe, "gt", i)
                        n = 512 if i == 0 else NG - 512
                        pe.matmul(ps("gt", i)[0:NH, 0:n], relb[:, :], oneh[:, 512 * i:512 * i + n],
                                  start=True, stop=True).then_inc(aux_done, 1)
                elif k == "mg":
                    _, c, q = s
                    what, i = CHUNKS[c]
                    if q == 0:
                        pe.wait_ge(w_lo_ready, c + 1)
                        if c in POOL_LO:
                            pe.wait_ge(pool_lo_ready, POOL_LO.index(c) + 1)
                    if c == 0 and q == 0:
                        for t in range(NT):
                            for g in range(2):
                                evacuated(pe, "hT", t, g)
                    if what in ("iq", "xbc", "conv"):
                        key = ("cg" if q < 2 else "ca", i) if what == "conv" else \
                            (what, 2 * i + q // 2)
                        if q % 2 == 0:
                            claim(pe, *key)
                        ks = range(4 * (q % 2), 4 * (q % 2) + 4)
                        ins = channels(c, q // 2, ps(*key)[:, :], ks)
                        if q % 2:
                            ins.then_inc(acc_step, 1)
                        continue
                    w_h, w_l = (w[:, c % NSLOT, :].rearrange("p (k n) -> p k n", k=4)
                                for w in (whi, wlo))
                    whole = what == "out"
                    if whole:
                        g, half = i
                        m_h, m_l = MIX[g]
                        key, k0 = ("wo", g, half, q), 0
                        if half == 0 and g != "conv":
                            evacuated(pe, "pv" if g == "att" else "yT", q)
                        elif (half, q) == (0, 0):
                            pe.wait_ge(clo_ready, 4)
                    else:
                        m_h, m_l = hhi, hlo
                        key, k0 = (what, q), 4 * i
                    if whole or i == 0:
                        claim(pe, *key)
                    f = slice(P * q, P * q + P)
                    ins = product(ps(*key)[:, :], [(m_h[:, k0 + kk, f],
                                                    conv_lo[:, q, kk, :] if m_l is conv_lo
                                                    else m_l[:, k0 + kk, f],
                                                    w_h[:, kk, :], w_l[:, kk, :])
                                                   for kk in range(4)],
                                  first=whole or i == 0, last=whole or i == 1)
                    if whole or i == 1 or q == 3:
                        ins.then_inc(acc_step, 1)
                elif k == "tbias":
                    pe.wait_ge(s_trev, 16)
                    claim(pe, *s)
                    pe.matmul(ps(*s)[:, :], jrev[:, :], trev[:, s[1], :], start=True, stop=True)\
                        .then_inc(aux_done, 1)
                elif k == "idx":
                    _, b, h = s
                    r = slice(ID * (h % 2), ID * (h % 2) + ID)
                    evacuated(pe, "ik", 0)
                    evacuated(pe, "iq", h // 2)
                    claim(pe, *s)
                    pe.matmul(ps(*s)[:, 0:P * (b + 1)], iqT[r, h // 2, P * b:P * b + P],
                              ikT[r, 0:P * (b + 1)], start=True, stop=True).then_inc(aux_done, 1)
                elif k == "qkT":
                    tok = q_tok if s[1] == "q" else k_tok
                    pe.wait_ge(qkn_ready, NT * ("qk".index(s[1]) + 1))
                    claim(pe, *s)
                    for t in range(NT):
                        ins = turn(ps(*s)[:, P * t:P * t + P], tok[:, t, P * s[2]:P * s[2] + P])
                    ins.then_inc(aux_done, 1)
                elif k == "score":
                    _, i, b, h = s
                    r = slice(HD * (h % 2), HD * (h % 2) + HD)
                    evacuated(pe, "qkT", "q", h // 2)
                    evacuated(pe, "qkT", "k", h // 2)
                    claim(pe, *s)
                    pe.matmul(ps(*s)[:, 0:P * (b + 1)], qT[r, h // 2, P * b:P * b + P],
                              kT[r, h // 2, 0:P * (b + 1)], start=True, stop=True)\
                        .then_inc(aux_done, 1)
                elif k == "turn":
                    _, i, b, h = s
                    pe.wait_ge(prob_ready, i + 1)
                    claim(pe, *s)
                    for j in range(b + 1):
                        ins = turn(ps(*s)[:, P * j:P * j + P], prob[:, i % 2, P * j:P * j + P])
                    ins.then_inc(aux_done, 1)
                elif k == "pv":
                    _, i, b, h = s
                    evacuated(pe, "turn", i, b, h)
                    if h == 0:
                        claim(pe, "pv", b)
                        for t in range(NT):
                            evacuated(pe, "v", t)
                    r = slice(HD * (h % 2), HD * (h % 2) + HD)
                    for j in range(b + 1):
                        ins = pe.matmul(ps("pv", b)[r, P * (h // 2):P * (h // 2) + P],
                                        v_tok[:, j, HD * h:HD * h + HD],
                                        probT[:, i % 2, P * j:P * j + P], start=j == 0, stop=j == b)
                    ins.then_inc(out_done, 1)
                elif k == "xt":
                    t = s[1]
                    pe.wait_ge(xbc_ready, 8)
                    claim(pe, "xs", t)
                    for j in range(4):
                        ins = turn(ps("xs", t)[:, P * j:P * j + P], xbcT[:, j, P * t:P * t + P])
                    ins.then_inc(aux_done, 1)
                elif k == "cs":
                    pe.wait_ge(dta_ready, 1)
                    claim(pe, "cs")
                    pe.matmul(ps("cs")[:, 0:32], tri[:, :], dta, start=True, stop=True)
                    pe.matmul(ps("cs")[:, 32:64], ones[:, :], dta, start=True, stop=True)\
                        .then_inc(aux_done, 1)
                elif k == "csr":
                    t = s[1]
                    for g in range(SG):
                        claim(pe, "csr", t, g)
                        for h in range(4):
                            c = SH * t + 4 * g + h
                            ins = pe.matmul(ps("csr", t, g)[:, P * h:P * h + P],
                                            dta[:, c:c + 1].to_broadcast([P, P]), tri[:, :],
                                            start=True, stop=True)
                        ins.then_inc(aux_done, 1)
                elif k == "ssd":
                    t = s[1]
                    q = slice(P * t, P * t + P)
                    claim(pe, "gt2", t)
                    for g in range(SG):
                        ins = pe.matmul(ps("gt2", t)[:, P * g:P * g + P], xbcT[:, 4 + g, q],
                                        xbcT[:, 6 + g, q], start=True, stop=True)
                    ins.then_inc(aux_done, 1)
                    if t < NT - 1:
                        claim(pe, "bt", t)
                        for g in range(SG):
                            ins = turn(ps("bt", t)[:, P * g:P * g + P], xbcT[:, 4 + g, q])
                        ins.then_inc(aux_done, 1)
                elif k == "yd":
                    t = s[1]
                    q = slice(P * t, P * t + P)
                    evacuated(pe, "gt2", t)
                    pe.wait_ge(xd_ready, 3 * t + 3)
                    claim(pe, "yd", t)
                    for h in range(SH):
                        c = slice(SP_ * h, SP_ * h + SP_)
                        ins = pe.matmul(ps("yd", t)[:, c], sct[:, h, :], xd[:, c], start=True,
                                        stop=True)
                    ins.then_inc(out_done, 1)
                    if t:
                        evacuated(pe, "st", t - 1)
                        claim(pe, "yo", t)
                        for g in range(SG):
                            c = slice(256 * g, 256 * g + 256)
                            ins = pe.matmul(ps("yo", t)[:, c], xbcT[:, 6 + g, q], state[:, c],
                                            start=True, stop=True)
                        ins.then_inc(aux_done, 1)
                    if t < NT - 1:
                        evacuated(pe, "bt", t)
                        claim(pe, "st", t)
                        for g in range(SG):
                            c = slice(256 * g, 256 * g + 256)
                            ins = pe.matmul(ps("st", t)[:, c], b_tok[:, t % 2, P * g:P * g + P],
                                            xdd[:, c], start=True, stop=True)
                        ins.then_inc(aux_done, 1)
                elif k == "yT":
                    t = s[1]
                    pe.wait_ge(yn_ready, t + 1)
                    claim(pe, "yT", t)
                    for j in range(4):
                        ins = turn(ps("yT", t)[:, P * j:P * j + P], yb[:, P * j:P * j + P])
                    ins.then_inc(aux_done, 1)
                elif k == "ln":
                    for j in range(4):
                        pe.wait_ge(dw_taps[j], CONV_K)
                    claim(pe, *s)
                    for j in range(4):
                        ins = turn(ps(*s)[:, P * j:P * j + P], u_acc[:, j, P * s[1]:P * s[1] + P])
                    ins.then_inc(aux_done, 1)
                elif k == "lnT":
                    for t in range(NT):
                        evacuated(pe, "ln", t)
                    claim(pe, *s)
                    for t in range(NT):
                        ins = turn(ps(*s)[:, P * t:P * t + P], u_tok[:, t, P * s[1]:P * s[1] + P])
                    ins.then_inc(aux_done, 1)

            for t in range(NT):
                for g in range(2):
                    evacuated(pe, "h2T", t, g)

            with pe.Fori(0, NF // 2) as n:
                for s in range(2):
                    c = UP0 + s
                    pe.wait_ge(w_lo_ready, n * 2 + (c + 1))
                    for v in range(2):
                        i = 2 * s + v
                        pe.wait_ge(drained[FFN_BANK[i]], n + ROUND0[i])
                        channels(c, v, bank[FFN_BANK[i]][:, :], range(KD)).then_inc(acc_step, 1)

            for j in range(NF // 2):
                c = DN0 + j
                pe.wait_ge(w_lo_ready, c + 1)
                pe.wait_ge(glo_ready, 2 * j + 3)
                w_h, w_l = (w[:, c % NSLOT, :].rearrange("p (k n) -> p k n", k=2)
                            for w in (whi, wlo))
                for t in range(NT):
                    q = slice(P * t, P * t + P)
                    for half in range(2):
                        f = slice(512 * half, 512 * half + 512)
                        b = DOWN_BANK[2 * t + half]
                        if j == 0:
                            pe.wait_ge(drained[b], DRAINS[b] + (NF // 2 if b < 4 else 0))
                        ins = product(bank[b][:, :],
                                      [(ghi[:, 2 * j + kk, q], glo[:, 2 * j + kk, q],
                                        w_h[:, kk, f], w_l[:, kk, f]) for kk in range(2)],
                                      first=j == 0, last=j == NF // 2 - 1)
                        if j == NF // 2 - 1 or (t, half) == (NT - 1, 1):
                            ins.then_inc(acc_step, 1)


_INS = ["x", "rel_bias", "norm_mix_g", "w_in", "conv_dw_w", "conv_dw_b", "conv_ln_g", "conv_ln_b",
        "q_norm_g", "k_norm_g", "ssm_conv_w", "ssm_conv_b", "dt_bias", "a_log", "d_skip",
        "ssm_norm_g", "w_out", "norm_ffn_g", "w_up", "ffn_conv_w", "ffn_conv_b", "w_down"]


def kernel(**inputs):
    import concourse.bacc as bacc
    from concourse.bass_utils import run_bass_kernel_spmd

    nc = bacc.Bacc("TRN2", target_bir_lowering=False, num_devices=1)
    arrays = {f"in_{n}": np.ascontiguousarray(inputs[n]) for n in _INS}
    arrays["in_onehot"] = bucket_onehot()
    args = [nc.dram_tensor(n, a.shape, mybir.dt.from_np(a.dtype), kind="ExternalInput").ap()
            for n, a in arrays.items()]
    out = nc.dram_tensor("out_x", (1, SEQ, DM), F32, kind="ExternalOutput").ap()
    build(nc, *args, out)
    r = run_bass_kernel_spmd(nc, [arrays], core_ids=[0])
    return r.results[0]["out_x"]
```
